# Optimizing a Trainium2 kernel written in Bass

```python
import math
import jax, jax.numpy as jnp
from jax import lax
import numpy as np

D_MODEL = 1024
BATCH = 1
SEQ = 512
DEPTH = 1
DEC_BATCH = 8
DEC_SEQ = 1
PAST_LEN = 4096
PAGE_SIZE = 128

D_MIX = D_MODEL
D_SSM = D_MIX // 2
D_GMLP = D_MIX - D_SSM
SSM_GROUP = 16
N_SSM_GROUPS = D_SSM // SSM_GROUP
SSM_STATE = 64
CHUNK = 128
N_GMLP_HEADS = 4
GMLP_HEAD = D_GMLP // N_GMLP_HEADS
N_EXPERT_GROUPS = 4
EXPERTS_PER_GROUP = 8
N_EXPERTS = N_EXPERT_GROUPS * EXPERTS_PER_GROUP
TOP_K_INNER = 2
D_EXPERT = D_MODEL // 2
D_IN = 2 * D_SSM + 2 * D_GMLP
EPS = 1e-6
DT_MIN = 1e-3
DT_MAX = 1e-1

kernel_name = 'hymba_s5_gmlp_hmoe_step'

def _rmsnorm(x, g):
    xf = x.astype(jnp.float32)
    y = xf * lax.rsqrt(jnp.mean(xf * xf, axis=-1, keepdims=True) + EPS) * g.astype(jnp.float32)
    return y.astype(x.dtype)

def _cplx_affine_combine(e1, e2):
    a1r, a1i, b1r, b1i = e1
    a2r, a2i, b2r, b2i = e2
    ar = a2r * a1r - a2i * a1i
    ai = a2r * a1i + a2i * a1r
    br = a2r * b1r - a2i * b1i + b2r
    bi = a2r * b1i + a2i * b1r + b2i
    return (ar, ai, br, bi)

def _ssm(xa, h0_re, h0_im, lam_re, lam_im, log_dt, b_re, b_im, c_re, c_im, d_skip):
    f32 = jnp.float32
    lam_re = lam_re.astype(f32)
    lam_im = lam_im.astype(f32)
    dt = jnp.exp(log_dt.astype(f32))[:, None]
    mag = jnp.exp(lam_re * dt)
    ang = lam_im * dt
    lb_re = mag * jnp.cos(ang)
    lb_im = mag * jnp.sin(ang)
    den = lam_re * lam_re + lam_im * lam_im
    nr = lb_re - 1.0
    ni = lb_im
    k_re = (nr * lam_re + ni * lam_im) / den
    k_im = (ni * lam_re - nr * lam_im) / den
    b_re = b_re.astype(f32)
    b_im = b_im.astype(f32)
    bb_re = k_re[:, :, None] * b_re - k_im[:, :, None] * b_im
    bb_im = k_re[:, :, None] * b_im + k_im[:, :, None] * b_re
    bu_re = jnp.einsum('nlgh,gph->nlgp', xa, bb_re)
    bu_im = jnp.einsum('nlgh,gph->nlgp', xa, bb_im)
    h0_re = h0_re.astype(f32)
    h0_im = h0_im.astype(f32)
    bu_re = bu_re.at[:, 0].add(lb_re * h0_re - lb_im * h0_im)
    bu_im = bu_im.at[:, 0].add(lb_re * h0_im + lb_im * h0_re)
    a_re = jnp.broadcast_to(lb_re, bu_re.shape)
    a_im = jnp.broadcast_to(lb_im, bu_im.shape)
    _, _, h_re, h_im = lax.associative_scan(_cplx_affine_combine, (a_re, a_im, bu_re, bu_im), axis=1)
    y = (jnp.einsum('nlgp,ghp->nlgh', h_re, c_re.astype(f32))
         - jnp.einsum('nlgp,ghp->nlgh', h_im, c_im.astype(f32))
         + d_skip.astype(f32) * xa)
    return y, h_re[:, -1], h_im[:, -1]

def _spatial_gate(v, w_s, b_s):
    n, l = v.shape[0], v.shape[1]
    n_chunks = -(-l // CHUNK)
    pad = n_chunks * CHUNK - l
    vp = jnp.pad(v, ((0, 0), (0, pad), (0, 0), (0, 0)))
    vp = vp.reshape(n, n_chunks, CHUNK, N_GMLP_HEADS, GMLP_HEAD)
    mask = jnp.tril(jnp.ones((CHUNK, CHUNK), dtype=bool))
    w = jnp.where(mask[None], w_s, jnp.zeros_like(w_s)).astype(v.dtype)
    s = jnp.einsum('hij,ncjhd->ncihd', w, vp) + jnp.transpose(b_s).astype(v.dtype)[None, None, :, :, None]
    return s.reshape(n, n_chunks * CHUNK, N_GMLP_HEADS, GMLP_HEAD)[:, :l]

def _moe(h, p):
    f32 = jnp.float32
    n, l, d = h.shape
    t = h.reshape(n * l, d)
    gl = (t @ p['w_router_group']).astype(f32) + p['b_router_group'].astype(f32)
    pg = jax.nn.softmax(gl, axis=-1)
    gi = jnp.argmax(gl, axis=-1)
    p_top = jnp.take_along_axis(pg, gi[:, None], axis=1)
    el = ((t @ p['w_router_expert']).astype(f32) + p['b_router_expert'].astype(f32))
    el = el.reshape(-1, N_EXPERT_GROUPS, EXPERTS_PER_GROUP)
    el_sel = jnp.take_along_axis(el, gi[:, None, None], axis=1)[:, 0]
    pe = jax.nn.softmax(el_sel, axis=-1)
    wv, wi = lax.top_k(pe, TOP_K_INNER)
    wv = wv / jnp.sum(wv, axis=-1, keepdims=True) * p_top
    eidx = gi[:, None] * EXPERTS_PER_GROUP + wi
    combine = jnp.einsum('tk,tke->te', wv, jax.nn.one_hot(eidx, N_EXPERTS, dtype=f32)).astype(t.dtype)
    out = jnp.zeros_like(t)
    for e in range(N_EXPERTS):
        a = t @ p['w_gate'][e]
        u = t @ p['w_up'][e]
        out = out + combine[:, e:e + 1] * ((jax.nn.silu(a) * u) @ p['w_down'][e])
    return out.reshape(n, l, d)

def _layer(x, h0_re, h0_im, p):
    n, l = x.shape[0], x.shape[1]
    dt = x.dtype
    hn = _rmsnorm(x, p['norm1_g'])
    z = hn @ p['w_in']
    xa, ga, ub, vb = jnp.split(z, [D_SSM, 2 * D_SSM, 2 * D_SSM + D_GMLP], axis=-1)
    xa_f = xa.astype(jnp.float32).reshape(n, l, N_SSM_GROUPS, SSM_GROUP)
    y_a, h_re, h_im = _ssm(xa_f, h0_re, h0_im, p['lam_re'], p['lam_im'], p['log_dt'],
                           p['ssm_b_re'], p['ssm_b_im'], p['ssm_c_re'], p['ssm_c_im'], p['ssm_d'])
    y_a = (jax.nn.gelu(y_a.reshape(n, l, D_SSM), approximate=False)
           * jax.nn.sigmoid(ga.astype(jnp.float32))).astype(dt)
    ub = jax.nn.gelu(ub, approximate=False)
    vb = jax.nn.gelu(vb, approximate=False).reshape(n, l, N_GMLP_HEADS, GMLP_HEAD)
    vb = _rmsnorm(vb, p['gmlp_norm_g'])
    s = _spatial_gate(vb, p['gmlp_w_s'], p['gmlp_b_s'])
    y_b = ub * s.reshape(n, l, D_GMLP)
    mix = jnp.concatenate([_rmsnorm(y_a, p['out_norm_ssm_g']), _rmsnorm(y_b, p['out_norm_gmlp_g'])], axis=-1)
    x = x + mix @ p['w_out']
    x = x + _moe(_rmsnorm(x, p['norm2_g']), p)
    return x, h_re, h_im, vb.reshape(n, l, D_GMLP)

def setup_inputs(seed: int = 0) -> dict:
    key = jax.random.key(seed)
    ks = jax.random.split(key, 32)
    f32 = jnp.float32
    nrm = lambda k, shape, scale: jax.random.normal(k, shape, f32) * scale
    n_idx = jnp.arange(SSM_STATE, dtype=f32)
    inp = {}
    inp['x_prompt'] = nrm(ks[0], (BATCH, SEQ, D_MODEL), 1.0)
    inp['x_sample'] = nrm(ks[1], (DEC_BATCH, DEC_SEQ, D_MODEL), 1.0)
    inp['state_ssm_re'] = nrm(ks[2], (DEPTH, DEC_BATCH, N_SSM_GROUPS, SSM_STATE), 0.5)
    inp['state_ssm_im'] = nrm(ks[3], (DEPTH, DEC_BATCH, N_SSM_GROUPS, SSM_STATE), 0.5)
    inp['norm1_g'] = 1.0 + nrm(ks[4], (DEPTH, D_MODEL), 0.01)
    inp['w_in'] = nrm(ks[5], (DEPTH, D_MODEL, D_IN), D_MODEL ** -0.5)
    inp['lam_re'] = -0.5 + nrm(ks[6], (DEPTH, N_SSM_GROUPS, SSM_STATE), 0.01)
    inp['lam_im'] = math.pi * n_idx + nrm(ks[7], (DEPTH, N_SSM_GROUPS, SSM_STATE), 0.01)
    inp['log_dt'] = jax.random.uniform(ks[8], (DEPTH, N_SSM_GROUPS), f32, math.log(DT_MIN), math.log(DT_MAX))
    inp['ssm_b_re'] = nrm(ks[9], (DEPTH, N_SSM_GROUPS, SSM_STATE, SSM_GROUP), (2 * SSM_GROUP) ** -0.5)
    inp['ssm_b_im'] = nrm(ks[10], (DEPTH, N_SSM_GROUPS, SSM_STATE, SSM_GROUP), (2 * SSM_GROUP) ** -0.5)
    inp['ssm_c_re'] = nrm(ks[11], (DEPTH, N_SSM_GROUPS, SSM_GROUP, SSM_STATE), (2 * SSM_STATE) ** -0.5)
    inp['ssm_c_im'] = nrm(ks[12], (DEPTH, N_SSM_GROUPS, SSM_GROUP, SSM_STATE), (2 * SSM_STATE) ** -0.5)
    inp['ssm_d'] = nrm(ks[13], (DEPTH, N_SSM_GROUPS, SSM_GROUP), 1.0)
    inp['gmlp_norm_g'] = 1.0 + nrm(ks[14], (DEPTH, N_GMLP_HEADS, GMLP_HEAD), 0.01)
    inp['gmlp_w_s'] = nrm(ks[15], (DEPTH, N_GMLP_HEADS, CHUNK, CHUNK), CHUNK ** -0.5)
    inp['gmlp_b_s'] = 1.0 + nrm(ks[16], (DEPTH, N_GMLP_HEADS, CHUNK), 0.1)
    inp['out_norm_ssm_g'] = 1.0 + nrm(ks[17], (DEPTH, D_SSM), 0.01)
    inp['out_norm_gmlp_g'] = 1.0 + nrm(ks[18], (DEPTH, D_GMLP), 0.01)
    inp['w_out'] = nrm(ks[19], (DEPTH, D_MIX, D_MODEL), D_MIX ** -0.5)
    inp['norm2_g'] = 1.0 + nrm(ks[20], (DEPTH, D_MODEL), 0.01)
    inp['w_router_group'] = nrm(ks[21], (DEPTH, D_MODEL, N_EXPERT_GROUPS), D_MODEL ** -0.5)
    inp['b_router_group'] = nrm(ks[22], (DEPTH, N_EXPERT_GROUPS), 0.01)
    inp['w_router_expert'] = nrm(ks[23], (DEPTH, D_MODEL, N_EXPERTS), D_MODEL ** -0.5)
    inp['b_router_expert'] = nrm(ks[24], (DEPTH, N_EXPERTS), 0.01)
    inp['w_gate'] = nrm(ks[25], (DEPTH, N_EXPERTS, D_MODEL, D_EXPERT), D_MODEL ** -0.5)
    inp['w_up'] = nrm(ks[26], (DEPTH, N_EXPERTS, D_MODEL, D_EXPERT), D_MODEL ** -0.5)
    inp['w_down'] = nrm(ks[27], (DEPTH, N_EXPERTS, D_EXPERT, D_MODEL), D_EXPERT ** -0.5)
    inp['final_norm_g'] = 1.0 + nrm(ks[28], (D_MODEL,), 0.01)
    return inp

def reference(x_prompt, x_sample, state_ssm_re, state_ssm_im, norm1_g, w_in, lam_re, lam_im, log_dt,
              ssm_b_re, ssm_b_im, ssm_c_re, ssm_c_im, ssm_d, gmlp_norm_g, gmlp_w_s, gmlp_b_s,
              out_norm_ssm_g, out_norm_gmlp_g, w_out, norm2_g, w_router_group, b_router_group,
              w_router_expert, b_router_expert, w_gate, w_up, w_down, final_norm_g):
    sdt = state_ssm_re.dtype
    xp = x_prompt
    xs = x_sample
    re_p, im_p, re_s, im_s, v_s = [], [], [], [], []
    zeros_state = jnp.zeros((x_prompt.shape[0], N_SSM_GROUPS, SSM_STATE), jnp.float32)
    for i in range(DEPTH):
        p = dict(norm1_g=norm1_g[i], w_in=w_in[i], lam_re=lam_re[i], lam_im=lam_im[i], log_dt=log_dt[i],
                 ssm_b_re=ssm_b_re[i], ssm_b_im=ssm_b_im[i], ssm_c_re=ssm_c_re[i], ssm_c_im=ssm_c_im[i],
                 ssm_d=ssm_d[i], gmlp_norm_g=gmlp_norm_g[i], gmlp_w_s=gmlp_w_s[i], gmlp_b_s=gmlp_b_s[i],
                 out_norm_ssm_g=out_norm_ssm_g[i], out_norm_gmlp_g=out_norm_gmlp_g[i], w_out=w_out[i],
                 norm2_g=norm2_g[i], w_router_group=w_router_group[i], b_router_group=b_router_group[i],
                 w_router_expert=w_router_expert[i], b_router_expert=b_router_expert[i],
                 w_gate=w_gate[i], w_up=w_up[i], w_down=w_down[i])
        xp, hr_p, hi_p, _ = _layer(xp, zeros_state, zeros_state, p)
        xs, hr_s, hi_s, vrows = _layer(xs, state_ssm_re[i], state_ssm_im[i], p)
        re_p.append(hr_p.astype(sdt))
        im_p.append(hi_p.astype(sdt))
        re_s.append(hr_s.astype(sdt))
        im_s.append(hi_s.astype(sdt))
        v_s.append(vrows)
    y_prompt = _rmsnorm(xp, final_norm_g)
    y_sample = _rmsnorm(xs, final_norm_g)
    return (y_prompt, y_sample, jnp.stack(re_p), jnp.stack(im_p), jnp.stack(re_s), jnp.stack(im_s), jnp.stack(v_s))


_drawn_inputs = setup_inputs


def setup_inputs(seed=0):
    import zlib

    import numpy as np

    out = dict(_drawn_inputs(seed))
    spreads = {}
    factors = {'norm1_g': 4.18,
     'lam_re': 4.241,
     'gmlp_norm_g': 5.839,
     'out_norm_ssm_g': 6.797,
     'out_norm_gmlp_g': 6.647,
     'norm2_g': 3.692,
     'b_router_group': 4.774,
     'b_router_expert': 5.1,
     'final_norm_g': 5.466}
    for name, (base, spread) in spreads.items():
        noise = np.random.default_rng([zlib.crc32(name.encode()), seed]).standard_normal(out[name].shape)
        drawn = base * np.exp(spread * noise) if base else spread * noise
        out[name] = __import__('jax').numpy.asarray(drawn.astype(out[name].dtype))
    for name, factor in factors.items():
        out[name] = (out[name] * factor).astype(out[name].dtype)
    return out
```

```python
import math
from contextlib import ExitStack

import concourse.bass as bass
from concourse import mybir

D = 1024
DS = 512
NP_, NS = 512, 8
NTOK = NP_ + NS
NT = 5
ROWS = [128, 128, 128, 128, NS]
KD = D // 128
NQ, NST = 16, 128
T = 4
NB = NP_ // T
UC = NB + 2 * NS
YC = NB + NS
NH, CH = 4, 128
NG, EPG, NE = 4, 8, 32
DE = 512
C = 64
MAXT = -(-NTOK // C)
NX = 2 * NTOK // (C + 1)
NTL = NE + NX
NSLOT, UNIT = 6, 4096
EPS = 1e-6
INVALID = 4000
TWO_PI = 2.0 * math.pi
MAGIC = 12582912.0
PI2_A = 6.28125
PI2_B = 0.0019350051879882812
PI2_C = TWO_PI - PI2_A - PI2_B
BIG = 1e38


def build(nc, a, o):
    f32, i32, bf16 = mybir.dt.float32, mybir.dt.int32, mybir.dt.bfloat16
    ALU, ACT, AX = mybir.AluOpType, mybir.ActivationFunctionType, mybir.AxisListType
    ctx = ExitStack()
    with ctx:
        def sb(name, shape, dt=f32):
            return ctx.enter_context(nc.sbuf_tensor(name, shape, dt))

        def sem(name):
            return ctx.enter_context(nc.semaphore(name))

        hn2_d = nc.dram_tensor("hn2_d", (NTOK, D), f32, kind="Internal").ap()
        tbl_d = nc.dram_tensor("tbl_d", (C * NTL, 2), i32, kind="Internal").ap()
        y2_d = nc.dram_tensor("y2_d", (2 * NTOK, D), f32, kind="Internal").ap()

        ring = sb("ring", [128, NSLOT, UNIT])
        arena = sb("arena", [128, 24928])

        def view(at, *shape):
            n = math.prod(shape)
            v = arena[:, at:at + n]
            names = "abcde"[:len(shape)]
            if len(shape) == 1:
                return v
            return v.rearrange(f"p ({' '.join(names)}) -> p {' '.join(names)}",
                               **dict(zip(names, shape)))

        def slot(s, *shape):
            n = math.prod(shape)
            names = "abcde"[:len(shape)]
            return ring[:, s, 0:n].rearrange(f"p ({' '.join(names)}) -> p {' '.join(names)}",
                                             **dict(zip(names, shape)))

        hnT = view(0, KD, NTOK)
        mixT = view(0, 8, NTOK)
        QT = view(4160, NQ, 2, 160)
        U = view(9280, NQ, UC)
        VH = view(11584, 2, NQ, UC)
        PTst = view(11584, NQ, 2, T, 32)
        T4 = view(16192, 4, 1024)
        uT = view(16192, 4, NTOK)
        sigT = view(20288, 4, NTOK)
        prod1 = view(20288, NQ, T, 16)
        prod2 = view(10560, NQ, T, 16)
        prodq1 = view(9280, NQ, 5, 16)
        sq = view(20288, 4, NTOK)
        vb = view(22368, 4, DS)
        vbs = view(24416, DS)
        PT = slot(3, NQ, 2, NST)
        rot = slot(4, 2, NQ, NB)
        MT = slot(5, NQ, 128)
        decay = ring[:, 5, 2048:3072]
        Ws = ring[:, 3, 0:512].rearrange("p (h j) -> p h j", h=NH)
        Bb = ring[:, 3, 512:1024].rearrange("p (r q h) -> p r q h", r=2, q=NQ)
        h0 = ring[:, 3, 1024:1280].rearrange("p (r s) -> p r s", r=2)
        lraw = ring[0:48, 3, 1280:1408]
        prodq2 = ring[:, 3, 2048:3328].rearrange("p (q e h) -> p q e h", q=NQ, e=5)
        xs4 = ring[:, 5, 3072:4096]
        zs = ring[:, 5, 3072:3584]
        hout = ring[:, 5, 3584:3968].rearrange("p (a s) -> p a s", a=3)
        Dd_all = T4[0:32, 3, 0:NQ * 32].rearrange("p (q n) -> p q n", q=NQ)
        x2 = view(4160, NT, D)
        hn2 = view(9280, 2, D)
        hn2T = view(11328, KD, 128)
        g2b = view(12352, D)
        gfb = view(13376, D)
        xg = view(14400, 2, D)
        xgT = view(16448, 2, KD, C)
        hT = view(17472, 2, 4, C)
        sg = view(17984, 2, DE)
        hh = view(19008, 2, DE)
        yst = view(0, 2, D)
        yin = view(20288, 2, 2, D)

        ident = sb("ident", [128, 128])
        sel = sb("sel", [128, NS])
        ldt = sb("ldt", [48, 2])
        lT = sb("lT", [128, 3, NQ])
        sc = sb("sc", [128, 16, NQ])
        Lp = sb("Lp", [128, 2, NQ, 5])
        Bc = sb("Bc", [128, 2, NQ, 16])
        Cr = view(22368, 2, 4, 128)
        CT = view(23392, 2, NQ, 16)
        h0T = sb("h0T", [128, 2, NS, NQ])
        hnew = sb("hnew", [128, 2, NS, NQ])
        hfin = sb("hfin", [128, 2, NQ])
        WT = sb("WT", [128, NH, 128])
        bsb = sb("bsb", [128, NH, 128])
        gmg = sb("gmg", [128, DS])
        w00 = sb("w00", [128, NH, 2])
        g1 = sb("g1", [128, KD])
        gab = sb("gab", [128, 8])
        Dc = sb("Dc", [32, NQ])
        st = sb("st", [128, 64])
        ss = sb("ss", [128, 4, 8])
        def small(at, *shape):
            return view(22368 + at, *shape)

        LG = small(0, NT, 36)
        eqb = small(180, NT, 32)
        cand = small(340, NT, 32)
        oh1 = small(500, NT, 32)
        oh2 = small(660, NT, 32)
        el2 = small(820, NT, 32)
        pre = small(980, NT, 32)
        wr = small(1140, KD, 36)
        brb = small(1428, 36)
        invt = arena[0:C, 24416:24416 + 2 * NTL].bitcast(i32)
        xxg = view(9280, D)
        xyst = view(10304, D)
        xsg = view(11328, DE)
        xhh = view(11840, DE)
        xxgT = view(12352, KD, C)
        xhT = view(12864, 4, C)
        rs = small(1496, 16, NT)
        cw = small(2160, 2, NT)
        fx = sb("fx", [128, NT])
        ohb = sb("ohb", [128, NT, 32], bf16)
        trib = sb("trib", [128, 128], bf16)
        oneb = sb("oneb", [128, 128], bf16)
        cnt = sb("cnt", [128, 48])
        iof = cnt[:, 0:32]
        xb = sb("xb", [1, NE + 1], i32)
        sloti = sb("sloti", [128, 2, NT], i32)
        rows = sb("rows", [128, NT, 2, 2], i32)
        tbl = small(1576, NTL, 2)[0:C].bitcast(i32)
        ig = small(1680, 2)[0:C].bitcast(i32)
        isc = small(1682, 2)[0:C].bitcast(i32)
        igx = small(1684, 2)[0:C].bitcast(i32)
        ones = sb("ones", [128, 2])
        sqb = view(11584, 4, NTOK)
        srow = view(13700, NTOK)[0:64]
        rab = sb("rab", [128, 5, 2])
        tsm = view(16192, 4, 512)[0:NS]
        psA = ctx.enter_context(nc.psum_tensor("psA", [128, 4, 512], f32))
        psB = ctx.enter_context(nc.psum_tensor("psB", [128, 4, 512], f32))

        x_in = [sem(f"x_in{t}") for t in range(NT)]
        w_full = [sem(f"w_full{s}") for s in range(NSLOT)]
        lam_in, bc_in, c_in, h0_in, ws_in, misc_in, g2_in, gf_in = map(
            sem, "lam_in bc_in c_in h0_in ws_in misc_in g2_in gf_in".split())
        st_out = sem("st_out")
        consts, zs_zero, u_zero, ws_masked, pool_step = map(
            sem, "consts zs_zero u_zero ws_masked pool_step".split())
        dve_step, act_step = sem("dve_step"), sem("act_step")
        lraw_rdy, lam_ps, ct_ps, wt_ps, h0_ps, small_ev = map(
            sem, "lraw_rdy lam_ps ct_ps wt_ps h0_ps small_ev".split())
        xsq, ms_rdy, rms_rdy, rstd_rdy, x_scaled, xT_ps, hn_copied = map(
            sem, "xsq ms_rdy rms_rdy rstd_rdy x_scaled xT_ps hn_copied".split())
        pre_v, pre_a = sem("pre_v"), sem("pre_a")
        lp_rdy, qt_rdy, rot_rdy, ptst_rdy = map(sem, "lp_rdy qt_rdy rot_rdy ptst_rdy".split())
        xa_ps, u_copied, zp_ps, zs_copied, zT_ps, zT_used = map(
            sem, "xa_ps u_copied zp_ps zs_copied zT_ps zT_used".split())
        in_ps, in_ev = sem("in_ps"), sem("in_ev")
        pt_ps, pt_copied, m_ps, m_copied, v_ps, v_copied = map(
            sem, "pt_ps pt_copied m_ps m_copied v_ps v_copied".split())
        turned_im, scanned, h_rdy, hout_ps, hout_copied = map(
            sem, "turned_im scanned h_rdy hout_ps hout_copied".split())
        y_ps, y_ev, ya_rdy, s_ps, yb_rdy, vbn, vbsn, vbsT_ps = map(
            sem, "y_ps y_ev ya_rdy s_ps yb_rdy vbn vbsn vbsT_ps".split())
        gq, gr = sem("gq"), sem("gr")
        sum_ps, srow_rdy, rab_ps, rab_ms, rab_rt, rab_rdy = map(
            sem, "sum_ps srow_rdy rab_ps rab_ms rab_rt rab_rdy".split())
        o_ps, o_ev, o_sc = sem("o_ps"), sem("o_ev"), sem("o_sc")
        n2sq, n2ms, n2rt, hn2_rdy, rest_in, hn2T_ps, hn2T_ev, lg_ps, lg_ev = map(
            sem, "n2sq n2ms n2rt hn2_rdy rest_in hn2T_ps hn2T_ev lg_ps lg_ev".split())
        hn2_out = [sem(f"hn2_out{u}") for u in range(2)]
        ex_in, ex_out, oh_rdy, pre_ps, slot_rdy, rows_rdy, tbl_init, tbl_set, xg_zero, inv_rdy = map(
            sem, "ex_in ex_out oh_rdy pre_ps slot_rdy rows_rdy tbl_init tbl_set xg_zero inv_rdy".split())
        gu_used, tbl_in, ig_rdy, is_rdy = map(sem, "gu_used tbl_in ig_rdy is_rdy".split())
        xx_ig, xx_in, xx_T, xx_Tev, xx_gu, xx_sg, xx_h, xx_hT, xx_hTev, xx_dn, xx_y0, xx_y1, xx_out = map(
            sem, ("xx_ig xx_in xx_T xx_Tev xx_gu xx_sg xx_h xx_hT xx_hTev xx_dn xx_y0 xx_y1 xx_out").split())
        xg_in = [sem(f"xg_in{u}") for u in range(2)]
        y_out = [sem(f"y_out{u}") for u in range(2)]
        xgT_ps, xgT_ev, gu_ps, sg_rdy, h_done, hT_ps, hT_ev, dn_ps, y0_ev, y1_ev = map(
            sem, "xgT_ps xgT_ev gu_ps sg_rdy h_done hT_ps hT_ev dn_ps y0_ev y1_ev".split())
        y_in = [sem(f"y_in{u}") for u in range(2)]
        f_sum, f_sq, f_ms, f_rt, f_done, f_out = map(sem, "f_sum f_sq f_ms f_rt f_done f_out".split())

        block = ctx.enter_context(nc.Block())

        w_in_q = a["w_in"][0].rearrange("(p k) n -> p k n", k=KD)
        w_out_v = a["w_out"][0].rearrange("(k p) n -> p k n", p=128)
        w_gate_v = a["w_gate"][0].rearrange("e (p k) n -> e p (k n)", p=128)
        w_up_v = a["w_up"][0].rearrange("e (p k) n -> e p (k n)", p=128)
        w_down_v = a["w_down"][0].rearrange("e (p k) n -> e p (k n)", p=128)
        XA, GA, UB, VB = range(4)
        EXP_SLOTS = [(3, 4, 5), (0, 1, 2)]
        PRIOR = [2, 2, 2, 0, 0, 0]

        def as8(s):
            return ring[:, s, :].rearrange("p (k n) -> p k n", k=KD)

        def as4(s):
            return ring[:, s, :].rearrange("p (k n) -> p k n", k=4)

        def by_pair(ps):
            return ps[:, :, :].rearrange("p a (b c) -> p (a b) c", c=256)

        def xrow(t):
            return T4[:, t, :] if t < 4 else xs4[0:NS]

        def xsrc(t):
            return (a["x_prompt"][0, t * 128:(t + 1) * 128, :] if t < 4
                    else a["x_sample"].rearrange("b l d -> (b l) d"))

        def stored(eng, n, u):
            if not isinstance(n, int) or n > 0:
                eng.wait_ge(y_out[u], n * 16)

        @block.sync
        def _(sp):
            def unit(s, src):
                sp.dma_start(src[0], src[1]).then_inc(w_full[s], 16)

            def w_in_unit(s, q):
                unit(s, (as8(s), w_in_q[:, :, q * 512:(q + 1) * 512]))

            for t in range(NT):
                sp.dma_start(xrow(t), xsrc(t)).then_inc(x_in[t], 16)
            w_in_unit(0, XA)
            w_in_unit(1, GA)
            w_in_unit(2, VB)
            sp.wait_ge(zT_ps, 1)
            w_in_unit(0, UB)
            sp.wait_ge(zT_ps, 2)
            unit(1, (as4(1), w_out_v[:, 0:4, :]))
            sp.wait_ge(zT_ps, 3)
            unit(2, (as4(2), w_out_v[:, 4:8, :]))
            sp.wait_ge(hout_copied, 1)
            for j, src in enumerate((hout[0:NQ, 0, :], hout[NQ:2 * NQ, 0, :], hout[:, 1, :], hout[:, 2, :])):
                sp.dma_start(o[2 + j][0].rearrange("b (q g) s -> (b q) (g s)", g=2), src).then_inc(st_out, 16)
            sp.wait_ge(vbn, NT)
            sp.dma_start(o[6].rearrange("o b l n -> (o b l) n"), vbs[0:NS]).then_inc(st_out, 16)
            sp.wait_ge(y_ps, 4)
            for t in range(NT):
                sp.dma_start(x2[0:ROWS[t], t, :], xsrc(t)).then_inc(x_in[t], 16)
            sp.wait_ge(st_out, 16 * 5)
            for s, w in zip(EXP_SLOTS[0], (w_gate_v, w_up_v, w_down_v)):
                unit(s, (ring[:, s, :], w[0]))
            sp.wait_ge(zT_ps, 4)
            unit(0, (ring[:, 0, :], w_gate_v[1]))
            for t in range(NT):
                sp.wait_ge(hn2_rdy, t + 1)
                sp.dma_start(hn2_d[t * 128:t * 128 + ROWS[t], :], hn2[0:ROWS[t], t % 2, :]).then_inc(hn2_out[t % 2], 16)
            sp.wait_ge(o_ps, NT)
            unit(1, (ring[:, 1, :], w_up_v[1]))
            unit(2, (ring[:, 2, :], w_down_v[1]))
            with sp.Fori(0, (NE - 2) // 2) as i:
                for u in range(2):
                    e = i * 2 + 2 + u
                    g, up, dn = EXP_SLOTS[u]
                    sp.wait_ge(gu_used, i * 2 + u + 1)
                    sp.dma_start(ring[:, g, :], w_gate_v[bass.ds(e, 1)].rearrange("e p n -> p (e n)")).then_inc(w_full[g], 16)
                    sp.dma_start(ring[:, up, :], w_up_v[bass.ds(e, 1)].rearrange("e p n -> p (e n)")).then_inc(w_full[up], 16)
                    sp.wait_ge(dn_ps, i * 2 + u + 1)
                    sp.dma_start(ring[:, dn, :], w_down_v[bass.ds(e, 1)].rearrange("e p n -> p (e n)")).then_inc(w_full[dn], 16)
            for u in range(2):
                sp.wait_ge(y_out[u], 16 * NE // 2)
            for t in range(NT):
                if t >= 2:
                    sp.wait_ge(f_done, t - 1)
                for c in range(2):
                    r0 = c * NTOK + t * 128
                    sp.dma_start(yin[0:ROWS[t], t % 2, c, :], y2_d[r0:r0 + ROWS[t], :]).then_inc(y_in[t % 2], 16)
            for t in range(NT):
                sp.wait_ge(f_done, t + 1)
                dst = o[0][0, t * 128:(t + 1) * 128, :] if t < 4 else o[1].rearrange("b l d -> (b l) d")
                sp.dma_start(dst, x2[0:ROWS[t], t, :]).then_inc(f_out, 16)
            sp.wait_ge(f_out, 16 * NT)

        @block.scalar
        def _(act):
            A = nc.scalar.activation
            steps = [0]

            def link(ins):
                steps[0] += 1
                ins.then_inc(act_step, 1)
                act.wait_ge(act_step, steps[0])

            pair_rows = lambda v: v[0].rearrange("(q g) s -> q (g s)", g=2)
            act.dma_start(lraw[0:NQ, :], pair_rows(a["lam_re"])).then_inc(lam_in, 16)
            act.dma_start(lraw[NQ:2 * NQ, :], pair_rows(a["lam_im"])).then_inc(lam_in, 16)
            act.dma_start(ldt[32:48, :], a["log_dt"][0].rearrange("(q g) -> q g", g=2)).then_inc(lam_in, 16)
            for r, n in enumerate(("ssm_c_re", "ssm_c_im")):
                v = a[n][0].rearrange("(t g) h s -> (g h) t s", t=4)
                for d in range(2):
                    act.dma_start(Cr[:, r, :, d * 64:(d + 1) * 64], v).then_inc(c_in, 16)
            act.dma_start(Ws, a["gmlp_w_s"][0].rearrange("h i j -> i h j")).then_inc(ws_in, 16)
            for r, n in enumerate(("state_ssm_re", "state_ssm_im")):
                act.dma_start(h0[:, r, :], a[n][0].rearrange("b (q g) s -> (b q) (g s)", g=2)).then_inc(h0_in, 16)
            for r, n in enumerate(("ssm_b_re", "ssm_b_im")):
                act.dma_start(Bb[:, r], a[n][0].rearrange("(q g) s h -> (g s) q h", g=2)).then_inc(bc_in, 16)
            act.dma_start(g1[:, :], a["norm1_g"][0].rearrange("(p k) -> p k", k=KD)).then_inc(misc_in, 16)
            act.dma_start(Dc[:, :], a["ssm_d"][0].rearrange("(q g) h -> (g h) q", g=2), allow_slow_non_contiguous=True).then_inc(misc_in, 16)
            for j, n in enumerate(("out_norm_ssm_g", "out_norm_gmlp_g")):
                act.dma_start(gab[:, 4 * j:4 * j + 4], a[n][0].rearrange("(m p) -> p m", p=128), allow_slow_non_contiguous=True).then_inc(misc_in, 16)
            act.dma_start(gmg[:, :], a["gmlp_norm_g"].rearrange("o h d -> o (h d)").to_broadcast([128, DS])).then_inc(misc_in, 16)
            act.dma_start(bsb[:, :, :].rearrange("p h i -> p (h i)"), a["gmlp_b_s"].rearrange("o h i -> o (h i)").to_broadcast([128, DS])).then_inc(misc_in, 16)
            act.dma_start(w00[:, :, 0:1], a["gmlp_w_s"][:, :, 0, 0:1].to_broadcast([128, NH, 1]), allow_slow_non_contiguous=True).then_inc(misc_in, 16)
            act.dma_start(w00[:, :, 1:2], a["gmlp_b_s"][:, :, 0:1].to_broadcast([128, NH, 1]), allow_slow_non_contiguous=True).then_inc(misc_in, 16)

            act.wait_ge(ms_rdy, 1)
            junk = [view(D * t, D) if t < 4 else view(20288, D) for t in range(NT)]
            for t in range(NT):
                act.wait_ge(x_in[t], 16)
                A(junk[t][0:ROWS[t]], xrow(t), ACT.Square, accum_out=st[0:ROWS[t], t:t + 1]).then_inc(xsq, 1)
            act.wait_ge(ms_rdy, 2)
            A(st[:, 8:13], st[:, 8:13], ACT.Sqrt).then_inc(rms_rdy, 1)
            act.wait_ge(rstd_rdy, 1)
            for t in range(NT):
                A(xrow(t), xrow(t), ACT.Copy, scale=st[0:ROWS[t], 16 + t:17 + t]).then_inc(x_scaled, 1)

            act.wait_ge(small_ev, 1)
            A(lT[:, 2, :], lT[:, 2, :], ACT.Exp).then_inc(pre_a, 1)
            act.wait_ge(pre_v, 1)
            A(sc[:, 1, :], sc[:, 0, :], ACT.Exp).then_inc(pre_a, 1)
            A(sc[:, 3, :], sc[:, 0, :], ACT.Exp, scale=4.0).then_inc(pre_a, 1)
            A(sc[:, 4, :], sc[:, 2, :], ACT.Sin).then_inc(pre_a, 1)
            A(sc[:, 5, :], sc[:, 2, :], ACT.Sin, scale=0.5).then_inc(pre_a, 1)

            def sample_copy(r):
                act.wait_ge(zp_ps, r + 1)
                for j in range(4):
                    ins = A(zs[32 * j:32 * j + NS], psA[32 * j:32 * j + NS, 0, :], ACT.Copy)
                ins.then_inc(zs_copied, 1)

            def u_copy(ql, e):
                src = psB[32 * ql:32 * ql + 32, :, :].rearrange("p m (b j) -> p j m b", j=T)[:, 3 - e]
                dst = U[32 * e:32 * e + 32, :, 0:NB].rearrange("p (m l) b -> p l m b", l=4)[:, ql]
                return dst, src

            act.wait_ge(zs_zero, 1)
            sample_copy(0)
            act.wait_ge(xa_ps, 4)
            act.wait_ge(qt_rdy, 1)
            act.wait_ge(ptst_rdy, 1)
            for e in range(T):
                for ql in range(2):
                    ins = A(*u_copy(ql, e), ACT.Copy)
            ins.then_inc(u_copied, 1)
            sample_copy(1)
            for m in range(4):
                act.wait_ge(in_ps, m + 1)
                if m == 0:
                    act.wait_ge(ptst_rdy, 1)
                A(sigT[:, m, 0:NP_], psA[:, 2 + m % 2, :], ACT.Sigmoid).then_inc(in_ev, 1)
            act.wait_ge(zT_ps, 2)
            A(sigT[:, :, NP_:NTOK], psA[:, 1, 0:32].rearrange("p (m n) -> p m n", m=4), ACT.Sigmoid).then_inc(zT_used, 1)
            sample_copy(2)
            for c in range(4):
                act.wait_ge(in_ps, 5 + c)
                if c == 0:
                    act.wait_ge(qt_rdy, 1)
                A(vb[:, c, :], psA[:, 2 + c % 2, :], ACT.Gelu).then_inc(in_ev, 1)
            act.wait_ge(zT_ps, 3)
            act.wait_ge(tbl_init, 16)
            A(vbs[0:NS], psA[0:NS, 1, :], ACT.Gelu).then_inc(zT_used, 1)
            for g in range(8):
                act.wait_ge(pt_ps, g + 1)
                A(PT[:, 2 * g:2 * g + 2, :, :].rearrange("p q r s -> p (q r s)"), psB[:, g % 4, :], ACT.Copy).then_inc(pt_copied, 1)
            for w in range(4):
                for r in range(2):
                    act.wait_ge(v_ps, 2 * w + r + 1)
                    A(VH[:, r, 4 * w:4 * w + 4, :], by_pair(psB)[:, 4 * r:4 * r + 4, 0:UC], ACT.Copy).then_inc(v_copied, 1)
            sample_copy(3)
            for m in range(4):
                act.wait_ge(in_ps, 9 + m)
                if m == 0:
                    act.wait_ge(h_rdy, 2)
                A(uT[:, m, 0:NP_], psA[:, 2 + m % 2, :], ACT.Gelu).then_inc(in_ev, 1)
            act.wait_ge(zT_ps, 4)
            A(uT[:, :, NP_:NTOK], psA[:, 1, 0:32].rearrange("p (m n) -> p m n", m=4), ACT.Gelu).then_inc(zT_used, 1)
            for ql in range(4):
                act.wait_ge(y_ps, ql + 1)
                for i in range(T):
                    dst = mixT[32 * ql:32 * ql + 32, 0:4, 0:NP_].rearrange("p m (b i) -> p i m b", i=T)[:, i]
                    bank = 2 * (ql % 2)
                    src = by_pair(psB)[32 * i:32 * i + 32, 2 * bank:2 * bank + 4, 0:NB]
                    A(dst, src, ACT.Gelu)
                src = by_pair(psB)[0:32, 2 * bank:2 * bank + 4, NB:YC]
                A(mixT[32 * ql:32 * ql + 32, 0:4, NP_:NTOK], src, ACT.Gelu).then_inc(y_ev, 1)
            for c in range(NT):
                act.wait_ge(gq, c + 1)
                r = 128 if c < 4 else NS
                A(st[0:r, 24 + 4 * c:28 + 4 * c], st[0:r, 24 + 4 * c:28 + 4 * c], ACT.Sqrt).then_inc(gr, 1)
            act.wait_ge(sum_ps, 1)
            A(srow[0:1, 0:NP_], psB[0:1, 2, :], ACT.Copy)
            A(srow[32:33, 0:NP_], psB[32:33, 2, :], ACT.Copy)
            A(srow[0:1, NP_:NTOK], psB[0:1, 3, 0:NS], ACT.Copy)
            A(srow[32:33, NP_:NTOK], psB[32:33, 3, 0:NS], ACT.Copy).then_inc(srow_rdy, 1)
            act.wait_ge(rab_ps, 1)
            act.dma_start(g2b, a["norm2_g"].to_broadcast([128, D])).then_inc(rest_in, 16)
            act.dma_start(gfb, a["final_norm_g"].unsqueeze(0).to_broadcast([128, D])).then_inc(rest_in, 16)
            act.dma_start(wr[:, :, 0:NG], a["w_router_group"][0].rearrange("(p k) n -> p k n", k=KD)).then_inc(rest_in, 16)
            act.dma_start(wr[:, :, NG:], a["w_router_expert"][0].rearrange("(p k) n -> p k n", k=KD)).then_inc(rest_in, 16)
            act.dma_start(brb[:, 0:NG], a["b_router_group"].to_broadcast([128, NG])).then_inc(rest_in, 16)
            act.dma_start(brb[:, NG:], a["b_router_expert"].to_broadcast([128, NE])).then_inc(rest_in, 16)
            act.wait_ge(rab_ms, 1)
            A(rab[:, :, :], rab[:, :, :], ACT.Sqrt).then_inc(rab_rt, 1)

            def norm2(t):
                r = ROWS[t]
                act.wait_ge(o_ev, t + 1)
                A(hn2[0:r, t % 2, :], x2[0:r, t, :], ACT.Square, accum_out=ss[0:r, 0, t:t + 1]).then_inc(n2sq, 1)
                act.wait_ge(n2ms, t + 1)
                A(ss[0:r, 1, t:t + 1], ss[0:r, 1, t:t + 1], ACT.Sqrt).then_inc(n2rt, 1)

            def hn2T_copy(t):
                act.wait_ge(hn2T_ps, t + 1)
                r = ROWS[t]
                ps = (psA, psB)[t % 2]
                A(hn2T[:, :, 0:r], ps[:, 0:2, :].rearrange("p a (b n) -> p (a b) n", n=128)[:, :, 0:r], ACT.Copy).then_inc(hn2T_ev, 1)

            for t in range(4):
                if t >= 2:
                    act.wait_ge(hn2_out[t % 2], 16)
                norm2(t)
                hn2T_copy(t)
            act.wait_ge(o_ps, NT)
            act.wait_ge(yb_rdy, 5)
            for g in range(4):
                ins = A(tsm[:, g, :], psA[32 * g:32 * g + NS, 0, :], ACT.Copy, scale=rab[32 * g:32 * g + NS, 4, 0:1])
            ins.then_inc(o_sc, 1)
            act.wait_ge(hn2_out[0], 32)
            norm2(4)
            hn2T_copy(4)
            act.wait_ge(ex_in, 1)
            A(cand[:, :, 0:NG], cand[:, :, 0:NG], ACT.Exp).then_inc(ex_out, 1)
            act.wait_ge(ex_in, 2)
            A(rs[:, 9, :], rs[:, 9, :], ACT.Exp).then_inc(ex_out, 1)

            act.wait_ge(slot_rdy, 1)

            def tile_step(s, i, u, first=False, last=False):
                ps, other = (psA, psB)[u], (psA, psB)[1 - u]
                act.wait_ge(gu_ps, s + 1)
                A(sg[64:128, u, :], ps[0:64, 1, :], ACT.Silu).then_inc(sg_rdy, 1)
                x0 = act.value_load(xb[0:1, bass.ds(s, 1)], min_val=0, max_val=NX)
                x1 = act.value_load(xb[0:1, bass.ds(s + 1, 1)], min_val=0, max_val=NX)
                with act.If(x0 < x1), act.Fori(x0, x1) as x:
                    act.wait_ge(xx_gu, x + 1)
                    A(xsg[64:128], other[0:64, 1, :], ACT.Silu).then_inc(xx_sg, 1)
                    act.wait_ge(xx_hT, x + 1)
                    A(xhT, other[:, 2, 0:256].rearrange("p (k c) -> p k c", k=4), ACT.Copy).then_inc(xx_hTev, 1)
                    act.wait_ge(xx_dn, x + 1)
                    A(xyst[0:C, 0:512], other[0:64, 0, :], ACT.Copy).then_inc(xx_y0, 1)
                if not first:
                    tail(s - 1, i, 1 - u)

            def tail(s, n_stored, u):
                ps = (psA, psB)[u]
                act.wait_ge(hT_ps, s + 1)
                A(hT[:, u, :, :], ps[:, 2, 0:256].rearrange("p (k c) -> p k c", k=4), ACT.Copy).then_inc(hT_ev, 1)
                act.wait_ge(dn_ps, s + 1)
                stored(act, n_stored, u)
                A(yst[0:C, u, 0:512], ps[0:64, 3, :], ACT.Copy).then_inc(y0_ev, 1)

            tile_step(0, 0, 0, first=True)
            tile_step(1, 0, 1)
            tile_step(2, 0, 0)
            with act.Fori(1, NE // 2 - 1) as i:
                tile_step(i * 2 + 1, i, 1)
                tile_step(i * 2 + 2, i, 0)
            tile_step(NE - 1, NE // 2 - 1, 1)
            tail(NE - 1, NE // 2 - 1, 1)
            for t in range(NT):
                r = ROWS[t]
                act.wait_ge(f_sum, t + 1)
                A(yin[0:r, t % 2, 0, :], x2[0:r, t, :], ACT.Square, accum_out=fx[0:r, t:t + 1]).then_inc(f_sq, 1)
                act.wait_ge(f_ms, t + 1)
                A(ss[0:r, 2, t:t + 1], ss[0:r, 2, t:t + 1], ACT.Sqrt).then_inc(f_rt, 1)

        @block.vector
        def _(dve):
            V = nc.vector
            steps = [0]

            def link(ins):
                steps[0] += 1
                ins.then_inc(dve_step, 1)
                dve.wait_ge(dve_step, steps[0])

            def tt(out, x, y, op):
                return V.tensor_tensor(out, x, y, op)

            V.memset(st[:, :], 1.0).then_inc(ms_rdy, 1)
            V.memset(rab[:, :, :], 1.0)
            link(V.memset(ss[:, :, :], 1.0))
            dve.wait_ge(lam_in, 48)
            link(V.tensor_copy(lraw[32:48, :].rearrange("q (g s) -> q g s", g=2),
                               ldt[32:48, :].unsqueeze(2).to_broadcast([NQ, 2, 64])))
            V.memset(Lp[:, 0, :, 0:1], 1.0).then_inc(lraw_rdy, 1)
            V.memset(Lp[:, 1, :, 0:1], 0.0)

            dve.wait_ge(xsq, NT)
            V.tensor_scalar(st[:, 8:13], st[:, 0:5], 1.0 / D, EPS, ALU.mult, ALU.add).then_inc(ms_rdy, 1)
            dve.wait_ge(rms_rdy, 1)
            V.reciprocal(st[:, 16:21], st[:, 8:13]).then_inc(rstd_rdy, 1)

            dve.wait_ge(lam_ps, 1)
            V.tensor_copy(lT[:, :, :], psB[:, 0, 0:48].rearrange("p (a q) -> p a q", a=3)).then_inc(small_ev, 1)
            dve.wait_ge(ct_ps, 1)
            for r in range(2):
                for par in range(2):
                    src = psB[:, 1 + r, :].rearrange("p (q g h) -> p g q h", g=2, h=16)[64 * par:64 * par + 64, par]
                    ins = V.tensor_copy(CT[64 * par:64 * par + 64, r], src)
            ins.then_inc(small_ev, 1)
            dve.wait_ge(wt_ps, 1)
            V.tensor_copy(WT[:, :, :].rearrange("p h i -> p (h i)"), psB[:, 3, :]).then_inc(small_ev, 1)
            dve.wait_ge(h0_ps, 1)
            V.tensor_copy(h0T[:, :, :, :].rearrange("p r n q -> p (r n q)"), psB[:, 0, 256:512]).then_inc(small_ev, 1)

            dve.wait_ge(misc_in, 16 * 8)
            for t in range(NT):
                dve.wait_ge(xT_ps, t + 1)
                r = ROWS[t]
                for j in range(2 if t < 4 else 1):
                    nk = 4 if t < 4 else 8
                    src = psA[:, 2 * (t % 2) + j, 0:nk * r].rearrange("p (k n) -> p k n", k=nk)
                    gain = g1[:, 4 * j:4 * j + nk].unsqueeze(2).to_broadcast([128, nk, r])
                    ins = tt(hnT[:, 4 * j:4 * j + nk, t * 128:t * 128 + r], src, gain, ALU.mult)
                ins.then_inc(hn_copied, 1)

            lr, li, dt = lT[:, 0, :], lT[:, 1, :], lT[:, 2, :]
            c = [sc[:, j, :] for j in range(16)]
            dve.wait_ge(pre_a, 1)
            tt(c[0], lr, dt, ALU.mult)
            link(tt(c[6], li, dt, ALU.mult))
            link(V.tensor_scalar(c[7], c[6], 1.0 / TWO_PI, MAGIC, ALU.mult, ALU.add))
            link(V.tensor_scalar(c[7], c[7], -MAGIC, None, ALU.add))
            for part in (PI2_A, PI2_B, PI2_C):
                link(V.scalar_tensor_tensor(c[6], c[7], -part, c[6], ALU.mult, ALU.add))
            V.tensor_scalar(c[2], c[6], 3.1415925, -3.1415925, ALU.min, ALU.max).then_inc(pre_v, 1)
            dve.wait_ge(pre_a, 5)
            link(tt(c[7], c[5], c[5], ALU.mult))
            link(V.tensor_scalar(c[7], c[7], -2.0, 1.0, ALU.mult, ALU.add))
            cos1, sin1 = c[7], c[4]
            tt(Lp[:, 0, :, 1], c[1], cos1, ALU.mult)
            link(tt(Lp[:, 1, :, 1], c[1], sin1, ALU.mult))

            def cmul(o_r, o_i, a_r, a_i, b_r, b_i, t1, t2):
                link(tt(t1, a_i, b_i, ALU.mult))
                link(tt(t2, a_r, b_r, ALU.mult))
                link(tt(o_r, t2, t1, ALU.subtract))
                link(tt(t1, a_r, b_i, ALU.mult))
                link(tt(t2, a_i, b_r, ALU.mult))
                link(tt(o_i, t1, t2, ALU.add))

            P = lambda r, e: Lp[:, r, :, e]
            cmul(P(0, 2), P(1, 2), P(0, 1), P(1, 1), P(0, 1), P(1, 1), c[8], c[9])
            cmul(P(0, 3), P(1, 3), P(0, 2), P(1, 2), P(0, 1), P(1, 1), c[8], c[9])
            cmul(P(0, 4), P(1, 4), P(0, 2), P(1, 2), P(0, 2), P(1, 2), c[8], c[9])
            cmul(c[10], c[11], cos1, sin1, cos1, sin1, c[8], c[9])
            cmul(rot[:, 0, :, 1], rot[:, 1, :, 1], c[10], c[11], c[10], c[11], c[8], c[9])
            link(V.memset(rot[:, 0, :, 0:1], 1.0))
            V.memset(rot[:, 1, :, 0:1], 0.0).then_inc(lp_rdy, 1)
            link(tt(c[8], lr, lr, ALU.mult))
            link(tt(c[9], li, li, ALU.mult))
            link(tt(c[8], c[8], c[9], ALU.add))
            link(V.reciprocal(c[12], c[8]))
            link(V.tensor_scalar(c[13], P(0, 1), -1.0, None, ALU.add))
            link(tt(c[8], c[13], lr, ALU.mult))
            link(tt(c[9], P(1, 1), li, ALU.mult))
            link(tt(c[8], c[8], c[9], ALU.add))
            link(tt(c[14], c[8], c[12], ALU.mult))
            link(tt(c[8], P(1, 1), lr, ALU.mult))
            link(tt(c[9], c[13], li, ALU.mult))
            link(tt(c[8], c[8], c[9], ALU.subtract))
            link(tt(c[15], c[8], c[12], ALU.mult))
            dve.wait_ge(bc_in, 32)
            k_r = c[14].unsqueeze(2).to_broadcast([128, NQ, 16])
            k_i = c[15].unsqueeze(2).to_broadcast([128, NQ, 16])
            b1 = prod1[:, :, 0, :]
            b2 = prod1[:, :, 1, :]
            cmul(Bc[:, 0], Bc[:, 1], k_r, k_i, Bb[:, 0], Bb[:, 1], b1, b2)
            dve.wait_ge(consts, 2)
            Lb = lambda r: Lp[:, r, :, 0:T].unsqueeze(3).to_broadcast([128, NQ, T, 16])
            Bx = lambda r: Bc[:, r].unsqueeze(2).to_broadcast([128, NQ, T, 16])
            for r in range(2):
                link(tt(prod1, Lb(0), Bx(r), ALU.mult))
                link(tt(prod2, Lb(1), Bx(1 - r), ALU.mult))
                for g in range(2):
                    h = slice(64 * g, 64 * g + 64)
                    ins = tt(PTst[h, :, r, :, 16 * g:16 * g + 16], prod1[h], prod2[h],
                             ALU.subtract if r == 0 else ALU.add)
                link(ins)
            V.memset(c[8], 0.0).then_inc(ptst_rdy, 1)

            def u_copy(ql, e):
                src = psB[32 * ql:32 * ql + 32, :, :].rearrange("p m (b j) -> p j m b", j=T)[:, 3 - e]
                dst = U[32 * e:32 * e + 32, :, 0:NB].rearrange("p (m l) b -> p l m b", l=4)[:, ql]
                return dst, src

            dve.wait_ge(xa_ps, 4)
            dve.wait_ge(qt_rdy, 1)
            for e in range(T):
                for ql in range(2, 4):
                    ins = V.tensor_copy(*u_copy(ql, e))
            ins.then_inc(u_copied, 1)
            dve.wait_ge(u_zero, 1)
            dve.wait_ge(zT_ps, 1)
            for e, at in ((3, NB), (0, NB + NS)):
                for ql in range(4):
                    src = psA[32 * ql:32 * ql + 32, 1, 0:32].rearrange("p (m n) -> p m n", m=4)
                    dst = U[32 * e:32 * e + 32, :, at:at + NS].rearrange("p (m l) n -> p l m n", l=4)[:, ql]
                    ins = V.tensor_copy(dst, src)
            ins.then_inc(zT_used, 1)

            link(tt(Dd_all, ident[0:32, 0:32].unsqueeze(1).to_broadcast([32, NQ, 32]),
                    Dc[:, :].unsqueeze(2).to_broadcast([32, NQ, 32]), ALU.mult))
            Mps = psB[0:32, :, :].rearrange("p a (b n) -> p (a b) n", n=128)
            dve.wait_ge(m_ps, 1)
            for e in range(T):
                blk = 32 * (3 - e)
                link(tt(MT[32 * e:32 * e + 32, :, blk:blk + 32], Mps[:, :, 0:32], Dd_all, ALU.add))
                if e:
                    ins = V.tensor_copy(MT[32 * e:32 * e + 32, :, blk + 32:128], Mps[:, :, 32:32 * (e + 1)])
                    link(ins)
            V.memset(c[9], 0.0).then_inc(m_copied, 1)

            q8 = lambda ap, h: ap[:, 8 * h:8 * h + 8]
            S = lambda j: T4[:, j, :].rearrange("p (q b) -> p q b", q=8)
            for h in range(2):
                cosb, sinb = q8(rot[:, 0], h), q8(rot[:, 1], h)
                Vr, Vi = q8(VH[:, 0], h)[:, :, 0:NB], q8(VH[:, 1], h)[:, :, 0:NB]
                dve.wait_ge(rot_rdy, 1)
                dec = decay.rearrange("p (q b) -> p q b", q=8)
                link(V.tensor_copy(dec, c[3][:, 8 * h:8 * h + 8].unsqueeze(2).to_broadcast([128, 8, NB])))
                link(V.memset(dec[:, :, 0:1], 0.0))
                dve.wait_ge(v_copied, 4 * (h + 1))
                link(tt(S(0), Vr, cosb, ALU.mult))
                link(tt(S(1), Vi, sinb, ALU.mult))
                link(tt(S(0), S(0), S(1), ALU.add))
                link(V.tensor_tensor_scan(T4[:, 1, :], decay, T4[:, 0, :], 0.0, ALU.mult, ALU.add))
                dve.wait_ge(turned_im, h + 1)
                link(V.tensor_tensor_scan(T4[:, 3, :], decay, T4[:, 2, :], 0.0, ALU.mult, ALU.add))
                Hr, Hi = q8(VH[:, 0], h), q8(VH[:, 1], h)
                for r, (H, x, y, op) in enumerate(((Hr, cosb, sinb, ALU.subtract), (Hi, sinb, cosb, ALU.add))):
                    link(tt(S(0), S(1), x, ALU.mult))
                    link(tt(S(2), S(3), y, ALU.mult))
                    tt(H[:, :, 1:NB], S(0)[:, :, 0:NB - 1], S(2)[:, :, 0:NB - 1], op)
                    link(tt(hfin[:, r, 8 * h:8 * h + 8], S(0)[:, :, NB - 1], S(2)[:, :, NB - 1], op))
                    V.memset(H[:, :, 0:1], 0.0)
                    link(V.tensor_copy(H[:, :, NB:NB + NS], h0T[:, r].rearrange("p n q -> p q n")[:, 8 * h:8 * h + 8]))
                if h == 1:
                    L1 = lambda r: Lp[:, r, :, 1].unsqueeze(1).to_broadcast([128, NS, NQ])
                    s1 = T4[:, 0, 0:128].rearrange("p (n q) -> p n q", n=NS)
                    s2 = T4[:, 1, 0:128].rearrange("p (n q) -> p n q", n=NS)
                    cmul(hnew[:, 0], hnew[:, 1], L1(0), L1(1), h0T[:, 0], h0T[:, 1], s1, s2)
                    for r in range(2):
                        link(tt(hnew[:, r], hnew[:, r], VH[:, r, :, NB + NS:UC].rearrange("p q n -> p n q"), ALU.add))
                V.memset(c[9], 0.0).then_inc(h_rdy, 1)

            def v_norm(t, tile, out_sem):
                r = ROWS[t]
                heads = lambda ap: ap.rearrange("p (h n) -> p h n", h=NH)
                scr = decay[0:r, 0:DS]
                m, rr = st[0:r, 24 + 4 * t:28 + 4 * t], st[0:r, 44 + 4 * t:48 + 4 * t]
                link(tt(scr, tile, tile, ALU.mult))
                link(V.tensor_reduce(m, heads(scr), AX.X, ALU.add))
                V.tensor_scalar(m, m, 1.0 / 128, EPS, ALU.mult, ALU.add).then_inc(gq, 1)
                link(tt(tile, tile, gmg[0:r], ALU.mult))
                dve.wait_ge(gr, t + 1)
                link(V.reciprocal(rr, m))
                tt(heads(tile), heads(tile), rr.unsqueeze(2).to_broadcast([r, NH, 128]), ALU.mult).then_inc(out_sem, 1)

            for t in range(4):
                dve.wait_ge(in_ev, 5 + t)
                v_norm(t, vb[:, t, :], vbn)
            dve.wait_ge(zT_used, 3)
            v_norm(4, vbs[0:NS], vbn)
            dve.wait_ge(hout_ps, 1)
            V.tensor_copy(hout[0:32, 0, :], psA[0:32, 0, 0:128])
            V.tensor_copy(hout[:, 1:3, :], psA[:, 0, 128:384].rearrange("p (r s) -> p r s", r=2)).then_inc(hout_copied, 1)

            dve.wait_ge(y_ev, 4)
            dve.wait_ge(zT_used, 4)
            ya = mixT[:, 0:4, :]
            link(tt(ya, ya, sigT, ALU.mult))
            link(tt(sq, ya, ya, ALU.mult))
            tt(ya, ya, gab[:, 0:4].unsqueeze(2).to_broadcast([128, 4, NTOK]), ALU.mult).then_inc(ya_rdy, 1)
            for h in range(NH):
                yb = mixT[:, 4 + h, 0:NP_]
                dve.wait_ge(s_ps, h + 1)
                link(tt(yb.rearrange("p (c i) -> p c i", c=4), psA[:, h, :].rearrange("p (c i) -> p c i", c=4),
                        bsb[:, h, :].unsqueeze(1).to_broadcast([128, 4, 128]), ALU.add))
                link(tt(yb, yb, uT[:, h, 0:NP_], ALU.mult))
                link(tt(sqb[:, h, 0:NP_], yb, yb, ALU.mult))
                V.tensor_scalar(yb, yb, gab[:, 4 + h:5 + h], None, ALU.mult).then_inc(yb_rdy, 1)
            ybs = mixT[:, 4:8, NP_:NTOK]
            dve.wait_ge(vbsT_ps, 1)
            link(tt(ybs, psB[:, 0, 0:32].rearrange("p (h n) -> p h n", h=4), w00[:, :, 0:1].to_broadcast([128, NH, NS]), ALU.mult))
            link(tt(ybs, ybs, w00[:, :, 1:2].to_broadcast([128, NH, NS]), ALU.add))
            link(tt(ybs, ybs, uT[:, :, NP_:NTOK], ALU.mult))
            link(tt(sqb[:, :, NP_:NTOK], ybs, ybs, ALU.mult))
            tt(ybs, ybs, gab[:, 4:8].unsqueeze(2).to_broadcast([128, NH, NS]), ALU.mult).then_inc(yb_rdy, 1)
            dve.wait_ge(rab_ps, 1)
            for j in range(2):
                V.tensor_copy(rab[:, 0:4, j], psB[:, 1 - j, 64:68])
            for g in range(4):
                ins = V.tensor_copy(rab[32 * g:32 * g + NS, 4, 0:1], psB[32 * g:32 * g + NS, 1 if g < 2 else 0, 68:69])
            link(ins)
            V.tensor_scalar(rab[:, :, :], rab[:, :, :], 1.0 / DS, EPS, ALU.mult, ALU.add).then_inc(rab_ms, 1)
            dve.wait_ge(rab_rt, 1)
            link(V.reciprocal(rab[:, :, :], rab[:, :, :]))
            V.memset(c[9], 0.0).then_inc(rab_rdy, 1)
            dve.wait_ge(rest_in, 16 * 6)
            V.memset(LG, 0.0)

            def normed(t):
                r = ROWS[t]
                dve.wait_ge(n2sq, t + 1)
                V.tensor_scalar(ss[0:r, 1, t:t + 1], ss[0:r, 0, t:t + 1], 1.0 / D, EPS, ALU.mult, ALU.add).then_inc(n2ms, 1)
                dve.wait_ge(n2rt, t + 1)
                link(V.reciprocal(ss[0:r, 3, t:t + 1], ss[0:r, 1, t:t + 1]))
                V.scalar_tensor_tensor(hn2[0:r, t % 2, :], x2[0:r, t, :], ss[0:r, 3, t:t + 1], g2b[0:r],
                                       ALU.mult, ALU.mult).then_inc(hn2_rdy, 1)

            def logits(t):
                r = ROWS[t]
                dve.wait_ge(lg_ps, t + 1)
                tt(LG[0:r, t, :], (psA, psB)[t % 2][0:r, 2, 0:36], brb[0:r], ALU.add).then_inc(lg_ev, 1)

            for t in range(4):
                ps = (psA, psB)[t % 2]
                dve.wait_ge(o_ps, t + 1)
                dve.wait_ge(x_in[t], 32)
                for j in range(2):
                    for h in range(2):
                        xh = x2[:, t, 512 * h:512 * h + 512]
                        link(V.scalar_tensor_tensor(xh, ps[:, 2 * j + h, :], rab[:, t, j:j + 1], xh, ALU.mult, ALU.add))
                V.memset(c[9], 0.0).then_inc(o_ev, 1)
                normed(t)
                if t:
                    logits(t - 1)
            dve.wait_ge(o_sc, 1)
            dve.wait_ge(x_in[4], 32)
            for j in range(2):
                link(tt(x2[0:NS, 4, :].rearrange("p (h n) -> p h n", h=2), x2[0:NS, 4, :].rearrange("p (h n) -> p h n", h=2),
                        tsm[:, 2 * j:2 * j + 2, :], ALU.add))
            V.memset(c[9], 0.0).then_inc(o_ev, 1)
            normed(4)
            logits(3)
            logits(4)

            R = lambda j: rs[:, j, :]
            def b(ap, n):
                return ap.unsqueeze(2).to_broadcast([128, NT, n])

            iota = iof[:, :].unsqueeze(1)

            def first_max(x, m, oh, n, scr):
                link(V.tensor_reduce(m, x, AX.X, ALU.max))
                link(tt(scr, x, b(m, n), ALU.is_ge))
                link(V.scalar_tensor_tensor(scr, scr, -1000.0, iota[:, :, 0:n].to_broadcast([128, NT, n]), ALU.mult, ALU.add))
                link(V.tensor_reduce(R(15), scr, AX.X, ALU.min))
                link(tt(oh, scr, b(R(15), n), ALU.is_equal))

            gl, el = LG[:, :, 0:NG], LG[:, :, NG:]
            ohg = oh1[:, :, 0:NG]
            dve.wait_ge(inv_rdy, 1)
            link(V.memset(c[9], 0.0))
            first_max(gl, R(0), ohg, NG, eqb[:, :, 0:NG])
            tt(cand[:, :, 0:NG], gl, b(R(0), NG), ALU.subtract).then_inc(ex_in, 1)
            dve.wait_ge(ex_out, 1)
            link(V.tensor_reduce(R(1), cand[:, :, 0:NG], AX.X, ALU.add))
            link(V.reciprocal(R(2), R(1)))
            link(V.tensor_scalar(eqb[:, :, 0:NG], ohg, -1.0, BIG, ALU.add, ALU.mult))
            link(tt(el2.rearrange("p t (g e) -> p t g e", g=NG), el.rearrange("p t (g e) -> p t g e", g=NG),
                    eqb[:, :, 0:NG].unsqueeze(3).to_broadcast([128, NT, NG, EPG]), ALU.add))
            first_max(el2, R(3), oh1, NE, cand)
            link(V.scalar_tensor_tensor(el2, oh1, -2.0 * BIG, el2, ALU.mult, ALU.add))
            first_max(el2, R(4), oh2, NE, cand)
            tt(R(9), R(4), R(3), ALU.subtract).then_inc(ex_in, 1)
            link(tt(eqb, oh1, oh2, ALU.add))
            V.tensor_copy(ohb[:, :, :], eqb).then_inc(oh_rdy, 1)
            dve.wait_ge(ex_out, 2)
            link(V.tensor_scalar(R(10), R(9), 1.0, None, ALU.add))
            link(V.reciprocal(R(10), R(10)))
            link(tt(cw[:, 0, :], R(10), R(2), ALU.mult))
            link(tt(cw[:, 1, :], cw[:, 0, :], R(9), ALU.mult))
            dve.wait_ge(pre_ps, 1)
            link(V.tensor_copy(pre, psA[:, 0, 0:NT * NE].rearrange("p (t e) -> p t e", t=NT)))
            cn, xt, xs = eqb[:, 0, :], eqb[:, 1, :], eqb[:, 2, :]
            link(V.tensor_copy(cn, psA[:, 1, 0:NE]))
            link(V.tensor_scalar(xt, cn, float(C), None, ALU.is_gt))
            for m in range(2, MAXT):
                link(V.scalar_tensor_tensor(xt, cn, float(C * m), xt, ALU.is_gt, ALU.add))
            link(V.memset(cn, 1.0))
            link(V.tensor_tensor_scan(xs, cn, xt, 0.0, ALU.mult, ALU.add))
            link(V.memset(xb[0:1, 0:1], 0))
            link(V.tensor_copy(xb[0:1, 1:NE + 1], xs[0:1]))
            link(tt(xs, xs, xt, ALU.subtract))
            for j, oh in enumerate((oh1, oh2)):
                link(tt(cand, oh, pre, ALU.mult))
                link(V.tensor_reduce(R(11), cand, AX.X, ALU.add))
                link(tt(cand, oh, iota.to_broadcast([128, NT, NE]), ALU.mult))
                link(V.tensor_reduce(R(12), cand, AX.X, ALU.add))
                link(tt(cand, oh, xs.unsqueeze(1).to_broadcast([128, NT, NE]), ALU.mult))
                link(V.tensor_reduce(R(14), cand, AX.X, ALU.add))
                link(V.tensor_scalar(R(13), R(11), float(C), None, ALU.is_ge))
                link(V.tensor_scalar(R(5), R(11), float(C), None, ALU.is_ge))
                for m in range(2, MAXT):
                    link(V.scalar_tensor_tensor(R(13), R(11), float(C * m), R(13), ALU.is_ge, ALU.add))
                link(V.scalar_tensor_tensor(R(14), R(14), float(NE - 1), R(13), ALU.add, ALU.add))
                link(tt(R(14), R(14), R(12), ALU.subtract))
                link(tt(R(14), R(14), R(5), ALU.mult))
                link(tt(R(14), R(14), R(12), ALU.add))
                link(V.scalar_tensor_tensor(R(11), R(13), float(-C), R(11), ALU.mult, ALU.add))
                link(V.scalar_tensor_tensor(R(11), R(11), float(NTL), R(14), ALU.mult, ALU.add))
                link(V.tensor_copy(sloti[:, j, :], R(11)))
            dve.wait_ge(hn2_out[0], 48)
            dve.wait_ge(hn2_out[1], 32)
            link(V.memset(xxg, 0.0))
            V.memset(xg, 0.0).then_inc(slot_rdy, 1)

            dve.wait_ge(slot_rdy, 1)

            def xT_copy(s, u):
                dve.wait_ge(xgT_ps, s + 1)
                V.tensor_copy(xgT[:, u].rearrange("p k c -> p (k c)"), (psA, psB)[u][:, 0, :]).then_inc(xgT_ev, 1)

            def tail(s, n_stored, u):
                dve.wait_ge(dn_ps, s + 1)
                stored(dve, n_stored, u)
                V.tensor_copy(yst[0:C, u, 512:1024], (psA, psB)[u][64:128, 3, :]).then_inc(y1_ev, 1)

            def tile_step(s, i, u, first=False, last=False):
                ps, other = (psA, psB)[u], (psA, psB)[1 - u]
                dve.wait_ge(sg_rdy, s + 1)
                V.tensor_tensor(hh[0:64, u, :], sg[64:128, u, :], ps[64:128, 1, :], ALU.mult).then_inc(h_done, 1)
                x0 = dve.value_load(xb[0:1, bass.ds(s, 1)], min_val=0, max_val=NX)
                x1 = dve.value_load(xb[0:1, bass.ds(s + 1, 1)], min_val=0, max_val=NX)
                with dve.If(x0 < x1), dve.Fori(x0, x1) as x:
                    dve.wait_ge(xx_T, x + 1)
                    V.tensor_copy(xxgT.rearrange("p k c -> p (k c)"), ps[:, 0, :]).then_inc(xx_Tev, 1)
                    dve.wait_ge(xx_sg, x + 1)
                    V.tensor_tensor(xhh[0:64], xsg[64:128], other[64:128, 1, :], ALU.mult).then_inc(xx_h, 1)
                    dve.wait_ge(xx_dn, x + 1)
                    V.tensor_copy(xyst[0:C, 512:1024], other[64:128, 0, :]).then_inc(xx_y1, 1)
                if not last:
                    xT_copy(s + 1, 1 - u)
                if not first:
                    tail(s - 1, i, 1 - u)

            xT_copy(0, 0)
            tile_step(0, 0, 0, first=True)
            tile_step(1, 0, 1)
            tile_step(2, 0, 0)
            with dve.Fori(1, NE // 2 - 1) as i:
                tile_step(i * 2 + 1, i, 1)
                tile_step(i * 2 + 2, i, 0)
            tile_step(NE - 1, NE // 2 - 1, 1, last=True)
            tail(NE - 1, NE // 2 - 1, 1)

            for t in range(NT):
                r = ROWS[t]
                dve.wait_ge(y_in[t % 2], 32 * (t // 2 + 1))
                for j in range(2):
                    link(V.scalar_tensor_tensor(x2[0:r, t, :], yin[0:r, t % 2, j, :], cw[0:r, j, t:t + 1], x2[0:r, t, :],
                                                ALU.mult, ALU.add))
                V.memset(c[9], 0.0).then_inc(f_sum, 1)
                dve.wait_ge(f_sq, t + 1)
                V.tensor_scalar(ss[0:r, 2, t:t + 1], fx[0:r, t:t + 1], 1.0 / D, EPS, ALU.mult, ALU.add).then_inc(f_ms, 1)
                dve.wait_ge(f_rt, t + 1)
                link(V.reciprocal(ss[0:r, 3, t:t + 1], ss[0:r, 2, t:t + 1]))
                V.scalar_tensor_tensor(x2[0:r, t, :], x2[0:r, t, :], ss[0:r, 3, t:t + 1], gfb[0:r],
                                       ALU.mult, ALU.mult).then_inc(f_done, 1)

        @block.gpsimd
        def _(pool):
            G = nc.gpsimd
            steps = [0]

            def link(ins):
                steps[0] += 1
                ins.then_inc(pool_step, 1)
                pool.wait_ge(pool_step, steps[0])

            def tt(out, x, y, op):
                return G.tensor_tensor(out, x, y, op)

            link(G.memset(ident[:, :], 0.0))
            link(G.affine_select(out=ident[:, :], in_=ident[:, :], compare_op=ALU.not_equal, fill=1.0, base=0,
                                 pattern=[[-1, 128]], channel_multiplier=1))
            G.memset(ones[:, :], 1.0)
            link(G.memset(sel[:, :], 0.0))
            for j in range(4):
                ins = G.tensor_copy(sel[32 * j:32 * j + NS, :], ident[32 * j:32 * j + NS, 32 * j:32 * j + NS])
            link(ins)
            G.memset(trib[:, :], 1.0).then_inc(consts, 1)
            pool.wait_ge(ws_in, 16)
            G.affine_select(out=Ws, in_=Ws, compare_op=ALU.is_ge, fill=0.0, base=0,
                            pattern=[[0, NH], [-1, 128]], channel_multiplier=1).then_inc(ws_masked, 1)
            link(G.memset(QT, 0.0))
            link(G.memset(MT, 0.0))
            G.memset(PTst, 0.0).then_inc(consts, 1)
            link(G.memset(invt, INVALID))
            pool.dma_start(tbl_d.rearrange("(p r) w -> p (r w)", p=C), invt).then_inc(tbl_init, 16)
            G.memset(oneb[:, :], 1.0)
            G.affine_select(out=trib[:, :], in_=trib[:, :], compare_op=ALU.is_gt, fill=0.0, base=0,
                            pattern=[[1, 128]], channel_multiplier=-1)
            G.iota(rows[:, :, :, 0], [[128, NT], [0, 2]], base=0, channel_multiplier=1)
            G.iota(rows[:, :, :, 1], [[128, NT], [NTOK, 2]], base=0, channel_multiplier=1)
            G.iota(iof, [[1, 32]], base=0, channel_multiplier=0, allow_small_or_imprecise_dtypes=True).then_inc(inv_rdy, 1)
            pool.wait_ge(xT_ps, NT)
            G.memset(zs, 0.0).then_inc(zs_zero, 1)

            pool.wait_ge(lp_rdy, 1)
            pool.wait_ge(small_ev, 2)
            Lb = lambda r: Lp[:, r].unsqueeze(3).to_broadcast([128, NQ, 5, 16])
            Cx = lambda r: CT[:, r].unsqueeze(2).to_broadcast([128, NQ, 5, 16])
            QTe = QT.rearrange("p q r (e n) -> p q r e n", e=5)
            for r in range(2):
                link(tt(prodq1, Lb(r), Cx(0), ALU.mult))
                link(tt(prodq2, Lb(1 - r), Cx(1), ALU.mult))
                if r:
                    link(G.tensor_scalar(prodq1, prodq1, -1.0, None, ALU.mult))
                for g in range(2):
                    h = slice(64 * g, 64 * g + 64)
                    ins = tt(QTe[h, :, r, :, 16 * g:16 * g + 16], prodq1[h], prodq2[h], ALU.subtract)
                link(ins)
            G.memset(fx[:, :], 1.0).then_inc(qt_rdy, 1)
            pool.wait_ge(ptst_rdy, 1)
            G.memset(U[:, :, NB:UC], 0.0).then_inc(u_zero, 1)

            m_r, m_i = T4[:, 2, 0:NQ], T4[:, 2, NQ:2 * NQ]
            s1, s2 = T4[:, 2, 2 * NQ:3 * NQ], T4[:, 2, 3 * NQ:4 * NQ]

            def cmul(o_r, o_i, a_r, a_i, b_r, b_i, t1, t2):
                link(tt(t1, a_i, b_i, ALU.mult))
                link(tt(t2, a_r, b_r, ALU.mult))
                link(tt(o_r, t2, t1, ALU.subtract))
                link(tt(t1, a_r, b_i, ALU.mult))
                link(tt(t2, a_i, b_r, ALU.mult))
                link(tt(o_i, t1, t2, ALU.add))

            w = 2
            while w < NB:
                cmul(m_r, m_i, rot[:, 0, :, w - 1], rot[:, 1, :, w - 1], rot[:, 0, :, 1], rot[:, 1, :, 1], s1, s2)
                t1 = T4[:, 0, 0:NQ * w].rearrange("p (q b) -> p q b", q=NQ)
                t2 = T4[:, 1, 0:NQ * w].rearrange("p (q b) -> p q b", q=NQ)
                cmul(rot[:, 0, :, w:2 * w], rot[:, 1, :, w:2 * w], rot[:, 0, :, 0:w], rot[:, 1, :, 0:w],
                     m_r.unsqueeze(2).to_broadcast([128, NQ, w]), m_i.unsqueeze(2).to_broadcast([128, NQ, w]), t1, t2)
                w *= 2
            G.memset(fx[:, :], 1.0).then_inc(rot_rdy, 1)

            for h in range(2):
                q8 = lambda ap: ap[:, 8 * h:8 * h + 8]
                S = lambda j: T4[:, j, :].rearrange("p (q b) -> p q b", q=8)
                pool.wait_ge(v_copied, 4 * (h + 1))
                if h:
                    pool.wait_ge(h_rdy, 1)
                link(tt(S(2), q8(VH[:, 1])[:, :, 0:NB], q8(rot[:, 0]), ALU.mult))
                link(tt(S(3), q8(VH[:, 0])[:, :, 0:NB], q8(rot[:, 1]), ALU.mult))
                tt(S(2), S(2), S(3), ALU.subtract).then_inc(turned_im, 1)

            pool.wait_ge(slot_rdy, 1)
            pool.wait_ge(tbl_init, 16)
            for t in range(NT):
                for j in range(2):
                    r = ROWS[t]
                    G.indirect_dma_start(out=tbl_d[:, :], out_offset=bass.IndirectOffsetOnAxis(ap=sloti[0:r, j, t:t + 1], axis=0),
                                         in_=rows[0:r, t, j, :], in_offset=None).then_inc(tbl_set, 16)
            pool.wait_ge(tbl_set, 16 * 2 * NT)
            pool.dma_start(tbl[:, :, :].rearrange("c t w -> c (t w)"),
                           tbl_d.rearrange("(c t) w -> c (t w)", c=C)).then_inc(tbl_in, 16)
            pool.wait_ge(tbl_in, 16)
            pool.wait_ge(hn2_out[0], 48)
            pool.wait_ge(hn2_out[1], 32)

            def gather(dst, rows_ap):
                return G.indirect_dma_start(out=dst, out_offset=None, in_=hn2_d[:, :],
                                            in_offset=bass.IndirectOffsetOnAxis(ap=rows_ap, axis=0),
                                            bounds_check=NTOK - 1, oob_is_err=False)

            def scatter(src, rows_ap):
                return G.indirect_dma_start(out=y2_d[:, :], out_offset=bass.IndirectOffsetOnAxis(ap=rows_ap, axis=0),
                                            in_=src, in_offset=None, bounds_check=2 * NTOK - 1, oob_is_err=False)

            def wait_before(signal, count):
                count = count if isinstance(count, int) else pool.to_reg(count)
                pool.wait_ge(tbl_in, 16)
                pool.wait_ge(signal, count)

            def fetch(s, u):
                G.tensor_copy(ig[:, u:u + 1], tbl[:, bass.ds(s, 1), 0]).then_inc(ig_rdy, 1)
                wait_before(ig_rdy, s + 1)
                gather(xg[0:C, u, :], ig[:, u:u + 1]).then_inc(xg_in[u], 16)

            def store(s, n_stored, u):
                stored(pool, n_stored, u)
                G.tensor_copy(isc[:, u:u + 1], tbl[:, bass.ds(s, 1), 1]).then_inc(is_rdy, 1)
                wait_before(y0_ev, s + 1)
                pool.wait_ge(y1_ev, s + 1)
                pool.wait_ge(is_rdy, s + 1)
                scatter(yst[0:C, u, :], isc[:, u:u + 1]).then_inc(y_out[u], 16)

            def tile_step(s, i, u, first=False, ahead=True):
                if ahead:
                    pool.wait_ge(xgT_ps, s + 1)
                    fetch(s + 2, u)
                x0 = pool.value_load(xb[0:1, bass.ds(s, 1)], min_val=0, max_val=NX)
                x1 = pool.value_load(xb[0:1, bass.ds(s + 1, 1)], min_val=0, max_val=NX)
                with pool.If(x0 < x1), pool.Fori(x0, x1) as x:
                    G.tensor_copy(igx[:, :], tbl[:, bass.ds(x + NE, 1), :].rearrange("c t w -> c (t w)")).then_inc(xx_ig, 1)
                    wait_before(xx_ig, x + 1)
                    gather(xxg[0:C, :], igx[:, 0:1]).then_inc(xx_in, 16)
                    wait_before(xx_y0, x + 1)
                    pool.wait_ge(xx_y1, x + 1)
                    scatter(xyst[0:C, :], igx[:, 1:2]).then_inc(xx_out, 16)
                    pool.wait_ge(xx_out, (x + 1) * 16)
                if not first:
                    store(s - 1, i, 1 - u)

            fetch(0, 0)
            fetch(1, 1)
            tile_step(0, 0, 0, first=True)
            tile_step(1, 0, 1)
            tile_step(2, 0, 0)
            with pool.Fori(1, NE // 2 - 2) as i:
                tile_step(i * 2 + 1, i, 1)
                tile_step(i * 2 + 2, i, 0)
            tile_step(NE - 3, NE // 2 - 2, 1)
            tile_step(NE - 2, NE // 2 - 2, 0, ahead=False)
            tile_step(NE - 1, NE // 2 - 1, 1, ahead=False)
            store(NE - 1, NE // 2 - 1, 1)

        @block.tensor
        def _(pe):
            def mm(out, lhsT, rhs, start, stop):
                return nc.tensor.matmul(out, lhsT, rhs, start=start, stop=stop, skip_group_check=True)

            def tr(out, in_):
                p = in_.shape[0]
                b0 = in_.base_partition() if callable(in_.base_partition) else in_.base_partition
                return nc.tensor.transpose(out, in_, ident[b0:b0 + p, b0:b0 + p])

            pe.wait_ge(consts, 1)
            pe.wait_ge(lraw_rdy, 1)
            tr(psB[:, 0, 0:48], lraw).then_inc(lam_ps, 1)
            pe.wait_ge(c_in, 64)
            for r in range(2):
                for t in range(4):
                    ins = tr(psB[:, 1 + r, 128 * t:128 * t + 128], Cr[:, r, t, :])
            ins.then_inc(ct_ps, 1)
            pe.wait_ge(ws_masked, 1)
            for h in range(NH):
                ins = tr(psB[:, 3, 128 * h:128 * h + 128], Ws[:, h, :])
            ins.then_inc(wt_ps, 1)
            pe.wait_ge(h0_in, 32)
            pe.wait_ge(small_ev, 1)
            for r in range(2):
                ins = tr(psB[:, 0, 256 + 128 * r:384 + 128 * r], h0[:, r, :])
            ins.then_inc(h0_ps, 1)

            for t in range(NT):
                r = ROWS[t]
                pe.wait_ge(x_scaled, t + 1)
                if t >= 2:
                    pe.wait_ge(hn_copied, t - 1)
                cols = xrow(t).rearrange("p (m k) -> p k m", k=KD)
                for k in range(KD):
                    if t < 4:
                        out = psA[:, 2 * (t % 2) + k // 4, 128 * (k % 4):128 * (k % 4) + 128]
                    else:
                        out = psA[:, 0, NS * k:NS * k + NS]
                    ins = tr(out, cols[:, k])
                ins.then_inc(xT_ps, 1)
            pe.wait_ge(hn_copied, NT)

            def partial(w):
                for k in range(KD):
                    j = k % 4
                    ins = mm(psA[32 * j:32 * j + NS, 0, :], hnT[:, k, NP_:NTOK], w[:, k, :], k < 4, k >= 4)
                ins.then_inc(zp_ps, 1)

            def total_T(r):
                pe.wait_ge(zs_copied, r + 1)
                if r:
                    pe.wait_ge(zT_used, r)
                for m in range(4):
                    ins = mm(psA[:, 1, NS * m:NS * m + NS], zs[:, 128 * m:128 * m + 128], sel[:, :], True, True)
                ins.then_inc(zT_ps, 1)

            pe.wait_ge(w_full[0], 16)
            partial(as8(0))
            pe.wait_ge(small_ev, 4)
            for m in range(4):
                for k in range(KD):
                    ins = mm(psB[:, m, :], as8(0)[:, k, 128 * m:128 * m + 128], hnT[:, k, 0:NP_], k == 0, k == KD - 1)
                ins.then_inc(xa_ps, 1)
            total_T(0)
            pe.wait_ge(w_full[1], 16)
            partial(as8(1))

            def to_T(w, first):
                for m in range(4):
                    if first + m >= 2:
                        pe.wait_ge(in_ev, first + m - 1)
                    for k in range(KD):
                        ins = mm(psA[:, 2 + m % 2, :], w[:, k, 128 * m:128 * m + 128], hnT[:, k, 0:NP_], k == 0, k == KD - 1)
                    ins.then_inc(in_ps, 1)

            to_T(as8(1), 0)
            total_T(1)
            pe.wait_ge(w_full[2], 16)
            partial(as8(2))
            for t in range(4):
                pe.wait_ge(in_ev, 3 + t)
                for k in range(KD):
                    ins = mm(psA[:, 2 + t % 2, :], hnT[:, k, 128 * t:128 * t + 128], as8(2)[:, k, :], k == 0, k == KD - 1)
                ins.then_inc(in_ps, 1)
            pe.wait_ge(zs_copied, 3)
            pe.wait_ge(zT_used, 2)
            mm(psA[0:NS, 1, :], sel[:, :], zs, True, True).then_inc(zT_ps, 1)

            pe.wait_ge(ptst_rdy, 1)
            pe.wait_ge(u_copied, 2)
            for g in range(8):
                if g >= 4:
                    pe.wait_ge(pt_copied, g - 3)
                for j in range(4):
                    q, r = 2 * g + j // 2, j % 2
                    ins = tr(psB[:, g % 4, 128 * j:128 * j + 128], PTst[:, q, r].rearrange("p e n -> p (e n)"))
                ins.then_inc(pt_ps, 1)
            pe.wait_ge(pt_copied, 8)
            pe.wait_ge(qt_rdy, 1)
            for q in range(NQ):
                out = psB[0:32, q // 4, 128 * (q % 4):128 * (q % 4) + 128]
                for r in range(2):
                    ins = mm(out, PTst[:, q, r, 0, :], QT[:, q, r, 0:128], r == 0, r == 1)
            ins.then_inc(m_ps, 1)
            pe.wait_ge(m_copied, 1)
            pe.wait_ge(zT_used, 1)
            for w in range(4):
                for r in range(2):
                    if w:
                        pe.wait_ge(v_copied, 2 * (w - 1) + r + 1)
                    for j in range(4):
                        ins = mm(by_pair(psB)[:, 4 * r + j, 0:UC], PT[:, 4 * w + j, r, :], U[:, 4 * w + j, :], True, True)
                    ins.then_inc(v_ps, 1)
            pe.wait_ge(w_full[0], 32)
            partial(as8(0))
            to_T(as8(0), 8)
            total_T(3)
            pe.wait_ge(h_rdy, 2)
            tr(psA[0:32, 0, 0:128], hfin[:, :, :].rearrange("p r q -> p (r q)"))
            for r in range(2):
                ins = tr(psA[:, 0, 128 + 128 * r:256 + 128 * r], hnew[:, r].rearrange("p n q -> p (n q)"))
            ins.then_inc(hout_ps, 1)
            for ql in range(4):
                if ql >= 2:
                    pe.wait_ge(y_ev, ql - 1)
                for m in range(4):
                    q = 4 * m + ql
                    out = by_pair(psB)[:, 4 * (ql % 2) + m, 0:YC]
                    mm(out, MT[:, q, :], U[:, q, 0:YC], True, False)
                    mm(out, QT[:, q, 0, 32:160], VH[:, 0, q, 0:YC], False, False)
                    ins = mm(out, QT[:, q, 1, 32:160], VH[:, 1, q, 0:YC], False, True)
                ins.then_inc(y_ps, 1)
            pe.wait_ge(vbn, NT)
            pe.wait_ge(hout_copied, 1)
            pe.wait_ge(in_ev, 12)
            pe.wait_ge(zT_used, 4)
            for h in range(NH):
                for t in range(4):
                    ins = mm(psA[:, h, 128 * t:128 * t + 128], vb[:, t, 128 * h:128 * h + 128], WT[:, h, :], True, True)
                ins.then_inc(s_ps, 1)
            pe.wait_ge(y_ev, 4)
            for h in range(NH):
                ins = tr(psB[:, 0, NS * h:NS * h + NS], vbs[0:NS, 128 * h:128 * h + 128])
            ins.then_inc(vbsT_ps, 1)

            wo = [as4(1), as4(2)]

            def out_proj(t):
                ps = (psA, psB)[t % 2]
                for j in range(2):
                    for h in range(2):
                        for k in range(4):
                            ins = mm(ps[:, 2 * j + h, :], mixT[:, 4 * j + k, 128 * t:128 * t + 128],
                                     wo[j][:, k, 512 * h:512 * h + 512], k == 0, k == 3)
                ins.then_inc(o_ps, 1)

            def router(t):
                r = ROWS[t]
                ps = (psA, psB)[t % 2]
                pe.wait_ge(o_ev, t + 1)
                pe.wait_ge(hn2_rdy, t + 1)
                cols = hn2[0:r, t % 2, :].rearrange("p (m k) -> p k m", k=KD)
                for k in range(KD):
                    ins = tr(ps[:, k // 4, 128 * (k % 4):128 * (k % 4) + r], cols[:, k])
                ins.then_inc(hn2T_ps, 1)
                pe.wait_ge(hn2T_ev, t + 1)
                for k in range(KD):
                    ins = mm(ps[0:r, 2, 0:36], hn2T[:, k, 0:r], wr[:, k, :], k == 0, k == KD - 1)
                ins.then_inc(lg_ps, 1)

            pe.wait_ge(w_full[1], 32)
            pe.wait_ge(w_full[2], 32)
            pe.wait_ge(ya_rdy, 1)
            pe.wait_ge(yb_rdy, 4)
            out_proj(0)
            pe.wait_ge(yb_rdy, 5)
            for k in range(4):
                for j, s in enumerate((sq, sqb)):
                    mm(psB[32 * j:32 * j + 1, 2, :], ones[:, 0:1], s[:, k, 0:NP_], k == 0, k == 3)
            for k in range(4):
                for j, s in enumerate((sq, sqb)):
                    ins = mm(psB[32 * j:32 * j + 1, 3, 0:NS], ones[:, 0:1], s[:, k, NP_:NTOK], k == 0, k == 3)
            ins.then_inc(sum_ps, 1)
            pe.wait_ge(srow_rdy, 1)
            for j in range(2):
                p = slice(32 * j, 32 * j + 1)
                for t in range(4):
                    mm(psB[:, 1 - j, 64 + t:65 + t], srow[p, 128 * t:128 * t + 128], ones[p, 0:1], True, True)
                for g in (2 * j, 2 * j + 1):
                    ins = mm(psB[32 * g:32 * g + NS, 1 - j, 68:69], srow[p, NP_:NTOK], ones[p, 0:1], True, True)
            ins.then_inc(rab_ps, 1)
            pe.wait_ge(rab_ms, 1)
            out_proj(1)
            pe.wait_ge(rest_in, 16 * 6)
            for t in range(2, 4):
                router(t - 2)
                pe.wait_ge(lg_ev, t - 1)
                out_proj(t)
            router(2)
            pe.wait_ge(lg_ev, 3)
            for k in range(4):
                for j in range(2):
                    for h in range(2):
                        g = 2 * j + h
                        ins = mm(psA[32 * g:32 * g + NS, 0, :], mixT[:, 4 * j + k, NP_:NTOK], wo[j][:, k, 512 * h:512 * h + 512], k == 0, k == 3)
            ins.then_inc(o_ps, 1)
            router(3)
            router(4)
            pe.wait_ge(oh_rdy, 1)
            for t in range(NT):
                out = psA[0:ROWS[t], 0, 32 * t:32 * t + 32]
                for s in range(t):
                    mm(out, oneb[:, 0:ROWS[t]], ohb[:, s, :], s == 0, False)
                mm(out, trib[0:ROWS[t], 0:ROWS[t]], ohb[0:ROWS[t], t, :], t == 0, True)
            for t in range(NT):
                ins = mm(psA[:, 1, 0:NE], oneb[0:ROWS[t], :], ohb[0:ROWS[t], t, :], t == 0, t == NT - 1)
            ins.then_inc(pre_ps, 1)

            pe.wait_ge(slot_rdy, 1)

            def x_T(out, x):
                cols = x.rearrange("p (m k) -> p k m", k=KD)
                for k in range(KD):
                    ins = tr(out[:, C * k:C * k + C], cols[:, k])
                return ins

            def gate_up(out, xT, g, up):
                for k in range(KD):
                    mm(out[0:64], xT[:, k, :], as8(g)[:, k, :], k == 0, k == KD - 1)
                    ins = mm(out[64:128], xT[:, k, :], as8(up)[:, k, :], k == 0, k == KD - 1)
                return ins

            def h_T(out, h):
                cols = h.rearrange("p (m k) -> p k m", k=4)
                for k in range(4):
                    ins = tr(out[:, C * k:C * k + C], cols[:, k])
                return ins

            def down(out, hT_, dn):
                for k in range(4):
                    for h in range(2):
                        ins = mm(out[64 * h:64 * h + 64], hT_[:, k, :], as4(dn)[:, k, 512 * h:512 * h + 512], k == 0, k == 3)
                return ins

            def wait_before(signal, count):
                count = count if isinstance(count, int) else pe.to_reg(count)
                pe.wait_ge(slot_rdy, 1)
                pe.wait_ge(signal, count)

            def tile_step(s, i, u, first=False, last=False):
                ps, other = (psA, psB)[u], (psA, psB)[1 - u]
                g, up, dn = EXP_SLOTS[u]
                pe.wait_ge(xgT_ev, s + 1)
                pe.wait_ge(w_full[g], (i + 1 + PRIOR[g]) * 16)
                pe.wait_ge(w_full[up], (i + 1 + PRIOR[up]) * 16)
                gate_up(ps[:, 1, :], xgT[:, u], g, up).then_inc(gu_ps, 1)
                x0 = pe.value_load(xb[0:1, bass.ds(s, 1)], min_val=0, max_val=NX)
                x1 = pe.value_load(xb[0:1, bass.ds(s + 1, 1)], min_val=0, max_val=NX)
                with pe.If(x0 < x1), pe.Fori(x0, x1) as x:
                    wait_before(xx_in, (x + 1) * 16)
                    x_T(ps[:, 0, :], xxg[0:C]).then_inc(xx_T, 1)
                    pe.wait_ge(xx_Tev, x + 1)
                    if not first:
                        pe.wait_ge(h_done, s)
                    gate_up(other[:, 1, :], xxgT, g, up).then_inc(xx_gu, 1)
                    wait_before(xx_h, x + 1)
                    h_T(other[:, 2, :], xhh[0:64]).then_inc(xx_hT, 1)
                    pe.wait_ge(xx_hTev, x + 1)
                    pe.wait_ge(w_full[dn], (i + 1 + PRIOR[dn]) * 16)
                    down(other[:, 0, :], xhT, dn).then_inc(xx_dn, 1)
                    pe.wait_ge(xx_y0, x + 1)
                    pe.wait_ge(xx_y1, x + 1)
                pe.drain().then_inc(gu_used, 1)
                if not first:
                    wait_before(h_done, s)
                    h_T(other[:, 2, :], hh[0:64, 1 - u, :]).then_inc(hT_ps, 1)
                if not last:
                    wait_before(xg_in[1 - u], (i + 1 + u) * 16)
                    x_T(other[:, 0, :], xg[0:C, 1 - u, :]).then_inc(xgT_ps, 1)
                if not first:
                    dnp = EXP_SLOTS[1 - u][2]
                    pe.wait_ge(hT_ev, s)
                    pe.wait_ge(w_full[dnp], (i + u + PRIOR[dnp]) * 16)
                    down(other[:, 3, :], hT[:, 1 - u], dnp).then_inc(dn_ps, 1)

            pe.wait_ge(xg_in[0], 16)
            x_T(psA[:, 0, :], xg[0:C, 0, :]).then_inc(xgT_ps, 1)
            tile_step(0, 0, 0, first=True)
            tile_step(1, 0, 1)
            tile_step(2, 1, 0)
            with pe.Fori(1, NE // 2 - 1) as i:
                tile_step(i * 2 + 1, i, 1)
                tile_step(i * 2 + 2, i + 1, 0)
            tile_step(NE - 1, NE // 2 - 1, 1, last=True)
            pe.wait_ge(h_done, NE)
            h_T(psB[:, 2, :], hh[0:64, 1, :]).then_inc(hT_ps, 1)
            pe.wait_ge(hT_ev, NE)
            pe.wait_ge(w_full[EXP_SLOTS[1][2]], (NE // 2 + PRIOR[EXP_SLOTS[1][2]]) * 16)
            down(psB[:, 3, :], hT[:, 1], EXP_SLOTS[1][2]).then_inc(dn_ps, 1)


_NAMES = ['x_prompt', 'x_sample', 'state_ssm_re', 'state_ssm_im', 'norm1_g', 'w_in', 'lam_re', 'lam_im', 'log_dt',
          'ssm_b_re', 'ssm_b_im', 'ssm_c_re', 'ssm_c_im', 'ssm_d', 'gmlp_norm_g', 'gmlp_w_s', 'gmlp_b_s',
          'out_norm_ssm_g', 'out_norm_gmlp_g', 'w_out', 'norm2_g', 'w_router_group', 'b_router_group',
          'w_router_expert', 'b_router_expert', 'w_gate', 'w_up', 'w_down', 'final_norm_g']
_OUTS = [(1, NP_, D), (NS, 1, D), (1, 1, 32, 64), (1, 1, 32, 64), (1, NS, 32, 64), (1, NS, 32, 64), (1, NS, 1, DS)]


def kernel(**inputs):
    import numpy as np
    import concourse.bacc as bacc
    from concourse.bass_utils import run_bass_kernel_spmd

    nc = bacc.Bacc("TRN2", target_bir_lowering=False, num_devices=1)
    arrays, args = {}, {}
    for name in _NAMES:
        v = np.ascontiguousarray(inputs[name])
        arrays[f"in_{name}"] = v
        args[name] = nc.dram_tensor(f"in_{name}", v.shape, mybir.dt.from_np(v.dtype), kind="ExternalInput").ap()
    outs = [nc.dram_tensor(f"out_{i}", s, mybir.dt.float32, kind="ExternalOutput").ap() for i, s in enumerate(_OUTS)]
    build(nc, args, outs)
    r = run_bass_kernel_spmd(nc, [arrays], core_ids=[0])
    return tuple(r.results[0][f"out_{i}"] for i in range(len(_OUTS)))
```

```python
import math
from contextlib import ExitStack

import concourse.bass as bass
from concourse import mybir

D = 1024
DS = 512
NP_, NS = 512, 8
NTOK = NP_ + NS
NT = 5
ROWS = [128, 128, 128, 128, NS]
KD = D // 128
NQ, NST = 16, 128
T = 4
NB = NP_ // T
UC = NB + 2 * NS
YC = NB + NS
NH = 4
NG, EPG, NE = 4, 8, 32
DE = 512
C = 64
NX = 2 * NTOK // C
NTL = NE + NX + 1
NSLOT, UNIT = 6, 4096
EPS = 1e-6
INVALID = 4000
TWO_PI = 2.0 * math.pi
MAGIC = 12582912.0
PI2_A = 6.28125
PI2_B = 0.0019350051879882812
PI2_C = TWO_PI - PI2_A - PI2_B
BIG = 1e38


def build(nc, a, o):
    f32, i32, bf16 = mybir.dt.float32, mybir.dt.int32, mybir.dt.bfloat16
    ALU, ACT, AX = mybir.AluOpType, mybir.ActivationFunctionType, mybir.AxisListType
    ctx = ExitStack()
    with ctx:
        def sb(name, shape, dt=f32):
            return ctx.enter_context(nc.sbuf_tensor(name, shape, dt))

        def sem(name):
            return ctx.enter_context(nc.semaphore(name))

        hn2_d = nc.dram_tensor("hn2_d", (NTOK, D), f32, kind="Internal").ap()
        y2_d = nc.dram_tensor("y2_d", (2 * NTOK, D), f32, kind="Internal").ap()

        ring = sb("ring", [128, NSLOT, UNIT])
        arena = sb("arena", [128, 24928])

        def view(at, *shape):
            n = math.prod(shape)
            v = arena[:, at:at + n]
            names = "abcde"[:len(shape)]
            if len(shape) == 1:
                return v
            return v.rearrange(f"p ({' '.join(names)}) -> p {' '.join(names)}",
                               **dict(zip(names, shape)))

        def slot(s, *shape):
            n = math.prod(shape)
            names = "abcde"[:len(shape)]
            return ring[:, s, 0:n].rearrange(f"p ({' '.join(names)}) -> p {' '.join(names)}",
                                             **dict(zip(names, shape)))

        hnT = view(0, KD, NTOK)
        mixT = view(0, 8, NTOK)
        QT = view(4160, NQ, 2, 160)
        U = view(9280, NQ, UC)
        VH = view(11584, 2, NQ, UC)
        PTst = view(11584, NQ, 2, T, 32)
        T4 = view(16192, 4, 1024)
        uT = slot(3, 4, NTOK)
        sigT = view(20288, 4, NTOK)
        prod1 = view(20288, NQ, T, 16)
        prod2 = view(19264, NQ, T, 16)
        prodq1 = view(16192, NQ, 5, 16)
        sq = view(20288, 4, NTOK)
        vb = view(22368, 4, DS)
        vbs = view(24416, DS)
        PT = slot(3, NQ, 2, NST)
        rot = slot(4, 2, NQ, NB)
        MT = slot(5, NQ, 128)
        decay = ring[:, 5, 2048:3072]
        Ws = ring[:, 3, 0:512].rearrange("p (h j) -> p h j", h=NH)
        Bb = ring[:, 3, 512:1024].rearrange("p (r q h) -> p r q h", r=2, q=NQ)
        h0 = ring[:, 3, 1024:1280].rearrange("p (r s) -> p r s", r=2)
        lraw = ring[0:48, 3, 1280:1408]
        prodq2 = ring[:, 3, 2048:3328].rearrange("p (q e h) -> p q e h", q=NQ, e=5)
        xs4 = ring[:, 5, 3072:4096]
        zs = ring[:, 5, 3072:3584]
        vsT = ring[:, 5, 3968:4000].rearrange("p (h n) -> p h n", h=NH)
        hout = ring[:, 5, 3584:3968].rearrange("p (a s) -> p a s", a=3)
        Dd_all = T4[0:32, 3, 0:NQ * 32].rearrange("p (q n) -> p q n", q=NQ)
        x2 = view(4160, NT, D)
        hn2 = view(9280, 2, D)
        hn2T = view(11328, KD, 128)
        g2b = view(12352, D)
        gfb = view(13376, D)
        xg = view(14400, 2, D)
        xgT = view(16448, 2, KD, C)
        hT = view(17472, 2, 4, C)
        sg = view(17984, 2, DE)
        hh = view(19008, 2, DE)
        yst = view(0, 2, D)
        early = (view(2112, 4, DE), view(20288, 4, DE))
        yin = ring[:, 0:3, :].rearrange("p s (c n) -> p (s c) n", n=D)

        ident = sb("ident", [128, 128])
        sel = sb("sel", [128, NS])
        ldt = sb("ldt", [48, 2])
        lT = sb("lT", [128, 3, NQ])
        sc = sb("sc", [128, 16, NQ])
        Lp = sb("Lp", [128, 2, NQ, 5])
        Bc = sb("Bc", [128, 2, NQ, 16])
        Cr = view(22368, 2, 4, 128)
        CT = view(23392, 2, NQ, 16)
        h0T = sb("h0T", [128, 2, NS, NQ])
        hnew = sb("hnew", [128, 2, NS, NQ])
        hfin = sb("hfin", [128, 2, NQ])
        WT = sb("WT", [128, NH, 128])
        bsb = sb("bsb", [128, NH, 128])
        gmg = sb("gmg", [128, DS])
        w00 = sb("w00", [128, NH, 2])
        g1 = sb("g1", [128, KD])
        gab = sb("gab", [128, 8])
        Dc = sb("Dc", [32, NQ])
        st = sb("st", [128, 64])
        ss = sb("ss", [128, 4, 8])
        def small(at, *shape):
            return view(22368 + at, *shape)

        LG = small(0, NT, 36)
        eqb = small(180, NT, 32)
        cand = small(340, NT, 32)
        oh1 = small(500, NT, 32)
        oh2 = small(660, NT, 32)
        el2 = small(820, NT, 32)
        wr = small(1140, KD, 36)
        brb = small(1428, 36)
        xxg = view(9280, D)
        xyst = view(10304, D)
        xsg = view(11328, DE)
        xhh = view(11840, DE)
        xxgT = view(12352, KD, C)
        xhT = view(12864, 4, C)
        rs = small(1496, 16, NT)
        oh12 = small(500, 2 * NT, 32)
        prod12 = view(16448, 2 * NT, 32)
        rs12 = view(16800, 8, 2 * NT)
        row_oh = view(16960, 2 * NT, C)
        tile_oh = view(17600, 2 * NT, NTL)
        entry = view(18100, 2 * NT, NTL, 2)
        vals = view(19100, 2, NT, 2)
        iot = view(19136, C)
        cw = small(2160, 2, NT)
        fx = sb("fx", [128, NT])
        ohb = sb("ohb", [128, NT, 32], bf16)
        trib = sb("trib", [128, 128], bf16)
        oneb = sb("oneb", [128, 128], bf16)
        iof = sb("iof", [128, NE])[:, :]
        xb = sb("xb", [1, NE + 1], i32)
        epsc = sb("epsc", [128, 1])
        tbl = small(1576, NTL, 2)[0:C].bitcast(i32)
        ig = small(1680, 2)[0:C].bitcast(i32)
        isc = small(1682, 2)[0:C].bitcast(i32)
        igx = small(1684, 2)[0:C].bitcast(i32)
        ones = sb("ones", [128, 2])
        sqb = view(16192, 4, NTOK)
        srow = view(18272, NTOK)[0:64]
        rab = sb("rab", [128, 5, 2])
        tsm = view(16192, 4, 512)[0:NS]
        psA = ctx.enter_context(nc.psum_tensor("psA", [128, 4, 512], f32))
        psB = ctx.enter_context(nc.psum_tensor("psB", [128, 4, 512], f32))

        x_in = [sem(f"x_in{t}") for t in range(NT)]
        w_full = [sem(f"w_full{s}") for s in range(NSLOT)]
        lam_in, bc_in, c_in, h0_in, ws_in, misc_in, g1_in = map(
            sem, "lam_in bc_in c_in h0_in ws_in misc_in g1_in".split())
        st_out = sem("st_out")
        consts, zs_zero, u_zero, ws_masked, pool_step = map(
            sem, "consts zs_zero u_zero ws_masked pool_step".split())
        dve_step, act_step = sem("dve_step"), sem("act_step")
        lraw_rdy, lam_ps, small_ps, small_ev = map(
            sem, "lraw_rdy lam_ps small_ps small_ev".split())
        xsq, ms_rdy, rms_rdy, x_scaled, xT_ps, hn_copied = map(
            sem, "xsq ms_rdy rms_rdy x_scaled xT_ps hn_copied".split())
        pre_v, pre_a = sem("pre_v"), sem("pre_a")
        lp_rdy, qt_rdy, rot_rdy, ptst_rdy = map(sem, "lp_rdy qt_rdy rot_rdy ptst_rdy".split())
        xa_ps, u_copied, zp_ps, zs_copied, zT_ps, zT_used = map(
            sem, "xa_ps u_copied zp_ps zs_copied zT_ps zT_used".split())
        in_ps, in_ev = sem("in_ps"), sem("in_ev")
        pt_ps, pt_copied, m_ps, m_copied, v_ps, v_copied = map(
            sem, "pt_ps pt_copied m_ps m_copied v_ps v_copied".split())
        turned_im, h_rdy, hout_ps, hout_copied = map(
            sem, "turned_im h_rdy hout_ps hout_copied".split())
        y_ps, y_ev, ya_rdy, s_ps, yb_rdy, vbn, sq_rdy = map(
            sem, "y_ps y_ev ya_rdy s_ps yb_rdy vbn sq_rdy".split())
        gq, gr = sem("gq"), sem("gr")
        sum_ps, srow_rdy, rab_ps, rab_ms, rab_rt = map(
            sem, "sum_ps srow_rdy rab_ps rab_ms rab_rt".split())
        o_ps, o_ev, o_sc = sem("o_ps"), sem("o_ev"), sem("o_sc")
        n2sq, n2rt, hn2_rdy, rest_in, hn2T_ps, hn2T_ev, lg_ps, lg_ev = map(
            sem, "n2sq n2rt hn2_rdy rest_in hn2T_ps hn2T_ev lg_ps lg_ev".split())
        hn2_out = [sem(f"hn2_out{u}") for u in range(2)]
        ex_in, ex_out, oh_rdy, pre_ps, slot_rdy, tbl_ps, tbl_rdy, iota_rdy, vals_rdy = map(
            sem, "ex_in ex_out oh_rdy pre_ps slot_rdy tbl_ps tbl_rdy iota_rdy vals_rdy".split())
        early_in, gu_used, ig_rdy, is_rdy = map(sem, "early_in gu_used ig_rdy is_rdy".split())
        xx_ig, xx_in, xx_T, xx_Tev, xx_gu, xx_sg, xx_h, xx_hT, xx_hTev, xx_dn, xx_y0, xx_y1, xx_out = map(
            sem, ("xx_ig xx_in xx_T xx_Tev xx_gu xx_sg xx_h xx_hT xx_hTev xx_dn xx_y0 xx_y1 xx_out").split())
        xg_in = [sem(f"xg_in{u}") for u in range(2)]
        y_out = [sem(f"y_out{u}") for u in range(2)]
        xgT_ps, xgT_ev, gu_ps, sg_rdy, h_done, hT_ps, hT_ev, dn_ps, y0_ev, y1_ev = map(
            sem, "xgT_ps xgT_ev gu_ps sg_rdy h_done hT_ps hT_ev dn_ps y0_ev y1_ev".split())
        y_in = [sem(f"y_in{t}") for t in range(NT)]
        f_scaled, f_first, f_sum, f_rt, f_done, f_out = map(sem, "f_scaled f_first f_sum f_rt f_done f_out".split())

        block = ctx.enter_context(nc.Block())

        w_in_q = a["w_in"][0].rearrange("(p k) n -> p k n", k=KD)
        w_out_v = a["w_out"][0].rearrange("(k p) n -> p k n", p=128)
        w_gate_v = a["w_gate"][0].rearrange("e (p k) n -> e p (k n)", p=128)
        w_up_v = a["w_up"][0].rearrange("e (p k) n -> e p (k n)", p=128)
        w_down_v = a["w_down"][0].rearrange("e (p k) n -> e p (k n)", p=128)
        XA, GA, UB, VB = range(4)
        EXP_SLOTS = [(3, 4, 5), (0, 1, 2)]
        ORDER = (0, 1, 2, 4, 3)
        LAST_ORDER = (4, 0, 1, 2, 3)
        PRIOR = [2, 2, 2, 0, 0, 0]

        def as8(s):
            return ring[:, s, :].rearrange("p (k n) -> p k n", k=KD)

        def as4(s):
            return ring[:, s, :].rearrange("p (k n) -> p k n", k=4)

        def by_pair(ps):
            return ps[:, :, :].rearrange("p a (b c) -> p (a b) c", c=256)

        def xrow(t):
            return T4[:, t, :] if t < 4 else xs4[0:NS]

        def xsrc(t):
            return (a["x_prompt"][0, t * 128:(t + 1) * 128, :] if t < 4
                    else a["x_sample"].rearrange("b l d -> (b l) d"))

        def u_copy(ql, e):
            src = psB[32 * ql:32 * ql + 32, :, :].rearrange("p m (b j) -> p j m b", j=T)[:, 3 - e]
            dst = U[32 * e:32 * e + 32, :, 0:NB].rearrange("p (m l) b -> p l m b", l=4)[:, ql]
            return dst, src

        def stored(eng, n, u):
            if not isinstance(n, int) or n > 0:
                eng.wait_ge(y_out[u], n * 16)

        @block.sync
        def _(sp):
            def unit(s, src):
                sp.dma_start(src[0], src[1]).then_inc(w_full[s], 16)

            def w_in_unit(s, q):
                unit(s, (as8(s), w_in_q[:, :, q * 512:(q + 1) * 512]))

            for t in range(NT):
                sp.dma_start(xrow(t), xsrc(t)).then_inc(x_in[t], 16)
            pair_rows = lambda v: v[0].rearrange("(q g) s -> q (g s)", g=2)
            sp.dma_start(lraw[0:NQ, :], pair_rows(a["lam_re"])).then_inc(lam_in, 16)
            sp.dma_start(lraw[NQ:2 * NQ, :], pair_rows(a["lam_im"])).then_inc(lam_in, 16)
            sp.dma_start(ldt[32:48, :], a["log_dt"][0].rearrange("(q g) -> q g", g=2)).then_inc(lam_in, 16)
            sp.dma_start(g1[:, :], a["norm1_g"][0].rearrange("(p k) -> p k", k=KD)).then_inc(g1_in, 16)
            w_in_unit(0, XA)
            for r, n in enumerate(("ssm_b_re", "ssm_b_im")):
                sp.dma_start(Bb[:, r], a[n][0].rearrange("(q g) s h -> (g s) q h", g=2)).then_inc(bc_in, 16)
            for r, n in enumerate(("ssm_c_re", "ssm_c_im")):
                v = a[n][0].rearrange("(t g) h s -> (g h) t s", t=4)
                for d in range(2):
                    sp.dma_start(Cr[:, r, :, d * 64:(d + 1) * 64], v).then_inc(c_in, 16)
            sp.dma_start(Ws, a["gmlp_w_s"][0].rearrange("h i j -> i h j")).then_inc(ws_in, 16)
            for r, n in enumerate(("state_ssm_re", "state_ssm_im")):
                sp.dma_start(h0[:, r, :], a[n][0].rearrange("b (q g) s -> (b q) (g s)", g=2)).then_inc(h0_in, 16)
            w_in_unit(1, GA)
            w_in_unit(2, VB)
            sp.dma_start(Dc[:, :], a["ssm_d"][0].rearrange("(q g) h -> (g h) q", g=2), allow_slow_non_contiguous=True).then_inc(misc_in, 16)
            for j, n in enumerate(("out_norm_ssm_g", "out_norm_gmlp_g")):
                sp.dma_start(gab[:, 4 * j:4 * j + 4], a[n][0].rearrange("(m p) -> p m", p=128), allow_slow_non_contiguous=True).then_inc(misc_in, 16)
            sp.dma_start(gmg[:, :], a["gmlp_norm_g"].rearrange("o h d -> o (h d)").to_broadcast([128, DS])).then_inc(misc_in, 16)
            sp.dma_start(bsb[:, :, :].rearrange("p h i -> p (h i)"), a["gmlp_b_s"].rearrange("o h i -> o (h i)").to_broadcast([128, DS])).then_inc(misc_in, 16)
            sp.dma_start(w00[:, :, 0:1], a["gmlp_w_s"][:, :, 0, 0:1].to_broadcast([128, NH, 1]), allow_slow_non_contiguous=True).then_inc(misc_in, 16)
            sp.dma_start(w00[:, :, 1:2], a["gmlp_b_s"][:, :, 0:1].to_broadcast([128, NH, 1]), allow_slow_non_contiguous=True).then_inc(misc_in, 16)
            sp.wait_ge(zT_ps, 1)
            w_in_unit(0, UB)
            sp.wait_ge(zT_ps, 2)
            unit(1, (as4(1), w_out_v[:, 0:4, :]))
            sp.wait_ge(zT_ps, 3)
            unit(2, (as4(2), w_out_v[:, 4:8, :]))
            sp.wait_ge(vbn, NT)
            sp.dma_start(o[6].rearrange("o b l n -> (o b l) n"), vbs[0:NS]).then_inc(st_out, 16)
            sp.wait_ge(hout_copied, 1)
            for j, src in enumerate((hout[0:NQ, 0, :], hout[NQ:2 * NQ, 0, :], hout[:, 1, :], hout[:, 2, :])):
                sp.dma_start(o[2 + j][0].rearrange("b (q g) s -> (b q) (g s)", g=2), src).then_inc(st_out, 16)
            sp.wait_ge(y_ps, 4)
            for t in range(NT):
                sp.dma_start(x2[0:ROWS[t], t, :], xsrc(t)).then_inc(x_in[t], 16)
            sp.wait_ge(s_ps, NH)
            sp.dma_start(g2b, a["norm2_g"].to_broadcast([128, D])).then_inc(rest_in, 16)
            sp.dma_start(gfb, a["final_norm_g"].unsqueeze(0).to_broadcast([128, D])).then_inc(rest_in, 16)
            sp.dma_start(wr[:, :, 0:NG], a["w_router_group"][0].rearrange("(p k) n -> p k n", k=KD)).then_inc(rest_in, 16)
            sp.dma_start(wr[:, :, NG:], a["w_router_expert"][0].rearrange("(p k) n -> p k n", k=KD)).then_inc(rest_in, 16)
            sp.dma_start(brb[:, 0:NG], a["b_router_group"].to_broadcast([128, NG])).then_inc(rest_in, 16)
            sp.dma_start(brb[:, NG:], a["b_router_expert"].to_broadcast([128, NE])).then_inc(rest_in, 16)
            sp.wait_ge(zT_ps, 4)
            unit(0, (ring[:, 0, :], w_gate_v[1]))
            sp.wait_ge(st_out, 16 * 5)
            sp.wait_ge(yb_rdy, 5)
            sp.wait_ge(sq_rdy, 9)
            for s, w in zip(EXP_SLOTS[0], (w_gate_v, w_up_v, w_down_v)):
                unit(s, (ring[:, s, :], w[0]))
            for n, t in enumerate(ORDER):
                sp.wait_ge(hn2_rdy, n + 1)
                sp.dma_start(hn2_d[t * 128:t * 128 + ROWS[t], :], hn2[0:ROWS[t], n % 2, :]).then_inc(hn2_out[n % 2], 16)
                if n == NT - 1:
                    sp.wait_ge(o_ps, NT)
            unit(1, (ring[:, 1, :], w_up_v[1]))
            unit(2, (ring[:, 2, :], w_down_v[1]))
            for j in range(2):
                sp.dma_start(early[j], w_gate_v[2][:, 2048 * j:2048 * j + 2048].rearrange("p (k n) -> p k n", k=4)).then_inc(early_in, 16)
            for e in range(2, 6):
                g, up, dn = EXP_SLOTS[e % 2]
                sp.wait_ge(gu_used, e - 1)
                if e % 2:
                    unit(g, (ring[:, g, :], w_gate_v[e]))
                unit(up, (ring[:, up, :], w_up_v[e]))
                if e == 2:
                    unit(g, (ring[:, g, :], w_gate_v[4]))
                sp.wait_ge(dn_ps, e - 1)
                unit(dn, (ring[:, dn, :], w_down_v[e]))
            with sp.Fori(2, (NE - 2) // 2) as i:
                for u in range(2):
                    e = i * 2 + 2 + u
                    g, up, dn = EXP_SLOTS[u]
                    sp.wait_ge(gu_used, i * 2 + u + 1)
                    sp.dma_start(ring[:, g, :], w_gate_v[bass.ds(e, 1)].rearrange("e p n -> p (e n)")).then_inc(w_full[g], 16)
                    sp.dma_start(ring[:, up, :], w_up_v[bass.ds(e, 1)].rearrange("e p n -> p (e n)")).then_inc(w_full[up], 16)
                    sp.wait_ge(dn_ps, i * 2 + u + 1)
                    sp.dma_start(ring[:, dn, :], w_down_v[bass.ds(e, 1)].rearrange("e p n -> p (e n)")).then_inc(w_full[dn], 16)
            for u in range(2):
                sp.wait_ge(y_out[u], 16 * NE // 2)
            for t in LAST_ORDER:
                for c in range(2):
                    r0 = c * NTOK + t * 128
                    sp.dma_start(yin[0:ROWS[t], 2 * t + c, :], y2_d[r0:r0 + ROWS[t], :]).then_inc(y_in[t], 16)
            for n, t in enumerate(LAST_ORDER):
                sp.wait_ge(f_done, n + 1)
                dst = o[0][0, t * 128:(t + 1) * 128, :] if t < 4 else o[1].rearrange("b l d -> (b l) d")
                sp.dma_start(dst, x2[0:ROWS[t], t, :]).then_inc(f_out, 16)
            sp.wait_ge(f_out, 16 * NT)

        @block.scalar
        def _(act):
            A = nc.scalar.activation
            steps = [0]

            def link(ins):
                steps[0] += 1
                ins.then_inc(act_step, 1)
                act.wait_ge(act_step, steps[0])

            act.wait_ge(ms_rdy, 1)
            A(st[:, 15:16], epsc[:, :], ACT.Sqrt)
            junk = [ring[:, 4, D * t:D * t + D] if t < 4 else view(20288, D) for t in range(NT)]

            def root(t):
                act.wait_ge(xsq, t + 1)
                r = ROWS[t]
                A(st[0:r, 8 + t:9 + t], st[0:r, t:t + 1], ACT.Sqrt, scale=1.0 / D, bias=epsc[0:r, :]).then_inc(rms_rdy, 1)

            for t in range(NT):
                act.wait_ge(x_in[t], 16)
                A(junk[t][0:ROWS[t]], xrow(t), ACT.Square, accum_out=st[0:ROWS[t], t:t + 1]).then_inc(xsq, 1)
                if t:
                    root(t - 1)
            root(NT - 1)

            act.wait_ge(small_ev, 1)
            A(lT[:, 2, :], lT[:, 2, :], ACT.Exp).then_inc(pre_a, 1)
            act.wait_ge(pre_v, 1)
            A(sc[:, 1, :], sc[:, 0, :], ACT.Exp).then_inc(pre_a, 1)
            A(sc[:, 3, :], sc[:, 0, :], ACT.Exp, scale=4.0).then_inc(pre_a, 1)
            A(sc[:, 4, :], sc[:, 2, :], ACT.Sin).then_inc(pre_a, 1)
            A(sc[:, 5, :], sc[:, 2, :], ACT.Sin, scale=0.5).then_inc(pre_a, 1)

            def sample_copy(r):
                act.wait_ge(zp_ps, r + 1)
                for j in range(4):
                    ins = A(zs[32 * j:32 * j + NS], psA[32 * j:32 * j + NS, 0, :], ACT.Copy)
                ins.then_inc(zs_copied, 1)

            act.wait_ge(zs_zero, 1)
            sample_copy(0)
            act.wait_ge(xa_ps, 4)
            for e in range(T):
                for ql in range(2):
                    ins = A(*u_copy(ql, e), ACT.Copy)
            ins.then_inc(u_copied, 1)
            sample_copy(1)
            for m in range(4):
                act.wait_ge(in_ps, m + 1)
                if m == 0:
                    act.wait_ge(ptst_rdy, 1)
                A(sigT[:, m, 0:NP_], psA[:, 2 + m % 2, :], ACT.Sigmoid).then_inc(in_ev, 1)
            act.wait_ge(zT_ps, 2)
            A(sigT[:, :, NP_:NTOK], psA[:, 1, 0:32].rearrange("p (m n) -> p m n", m=4), ACT.Sigmoid).then_inc(zT_used, 1)
            act.wait_ge(qt_rdy, 1)
            for g in range(8):
                act.wait_ge(pt_ps, g + 1)
                A(PT[:, 2 * g:2 * g + 2, :, :].rearrange("p q r s -> p (q r s)"), psB[:, g % 4, :], ACT.Copy).then_inc(pt_copied, 1)

            def v_gelu(c):
                act.wait_ge(in_ps, 5 + c)
                A(vb[:, c, :], psA[:, 2 + c % 2, :], ACT.Gelu).then_inc(in_ev, 1)

            sample_copy(2)
            act.wait_ge(qt_rdy, 1)
            v_gelu(0)
            for w in range(4):
                for r in range(2):
                    act.wait_ge(v_ps, 2 * w + r + 1)
                    A(VH[:, r, 4 * w:4 * w + 4, :], by_pair(psB)[:, 4 * r:4 * r + 4, 0:UC], ACT.Copy).then_inc(v_copied, 1)
            for c in range(1, 4):
                v_gelu(c)
            act.wait_ge(zT_ps, 3)
            A(vbs[0:NS], psA[0:NS, 1, :], ACT.Gelu).then_inc(zT_used, 1)
            sample_copy(3)
            for m in range(4):
                if m == 3:
                    act.wait_ge(gq, 1)
                    A(st[:, 24:44], st[:, 24:44], ACT.Sqrt).then_inc(gr, 1)
                act.wait_ge(in_ps, 9 + m)
                A(uT[:, m, 0:NP_], psA[:, 2 + m % 2, :], ACT.Gelu).then_inc(in_ev, 1)
            act.wait_ge(zT_ps, 4)
            A(uT[:, :, NP_:NTOK], psA[:, 1, 0:32].rearrange("p (m n) -> p m n", m=4), ACT.Gelu).then_inc(zT_used, 1)
            for ql in range(4):
                act.wait_ge(y_ps, ql + 1)
                for i in range(T):
                    dst = mixT[32 * ql:32 * ql + 32, 0:4, 0:NP_].rearrange("p m (b i) -> p i m b", i=T)[:, i]
                    bank = 2 * (ql % 2)
                    src = by_pair(psB)[32 * i:32 * i + 32, 2 * bank:2 * bank + 4, 0:NB]
                    A(dst, src, ACT.Gelu)
                src = by_pair(psB)[0:32, 2 * bank:2 * bank + 4, NB:YC]
                A(mixT[32 * ql:32 * ql + 32, 0:4, NP_:NTOK], src, ACT.Gelu).then_inc(y_ev, 1)
            for m in range(4):
                act.wait_ge(ya_rdy, m + 1)
                A(sq[:, m, :], sigT[:, m, :], ACT.Square).then_inc(sq_rdy, 1)
            for h in range(NH):
                act.wait_ge(yb_rdy, h + 1)
                A(sqb[:, h, 0:NP_], uT[:, h, 0:NP_], ACT.Square).then_inc(sq_rdy, 1)
            act.wait_ge(yb_rdy, 5)
            A(sqb[:, :, NP_:NTOK], uT[:, :, NP_:NTOK], ACT.Square).then_inc(sq_rdy, 1)
            act.wait_ge(sum_ps, 1)
            A(srow[0:1, 0:NP_], psA[0:1, 2, :], ACT.Copy)
            A(srow[32:33, 0:NP_], psA[32:33, 2, :], ACT.Copy)
            A(srow[0:1, NP_:NTOK], psA[0:1, 3, 0:NS], ACT.Copy)
            A(srow[32:33, NP_:NTOK], psA[32:33, 3, 0:NS], ACT.Copy).then_inc(srow_rdy, 1)
            act.wait_ge(rab_ms, 1)
            A(rab[:, :, :], rab[:, :, :], ACT.Sqrt).then_inc(rab_rt, 1)

            def norm2(n, t):
                r = ROWS[t]
                if n >= 2:
                    act.wait_ge(hn2_out[n % 2], 16 * (n // 2))
                act.wait_ge(o_ev, n + 1)
                A(hn2[0:r, n % 2, :], x2[0:r, t, :], ACT.Square, accum_out=ss[0:r, 0, t:t + 1]).then_inc(n2sq, 1)
                act.wait_ge(n2sq, n + 1)
                A(ss[0:r, 1, t:t + 1], ss[0:r, 0, t:t + 1], ACT.Sqrt, scale=1.0 / D, bias=epsc[0:r, :]).then_inc(n2rt, 1)

            def hn2T_copy(n, t):
                act.wait_ge(hn2T_ps, n + 1)
                r = ROWS[t]
                ps = (psB, psA)[t % 2]
                A(hn2T[:, :, 0:r], ps[:, 0:2, :].rearrange("p a (b n) -> p (a b) n", n=128)[:, :, 0:r], ACT.Copy).then_inc(hn2T_ev, 1)

            for n in range(3):
                norm2(n, n)
                if n < 2:
                    hn2T_copy(n, n)
            act.wait_ge(o_ps, 4)
            for g in range(4):
                ins = A(tsm[:, g, :], psA[32 * g:32 * g + NS, 3, :], ACT.Copy, scale=rab[32 * g:32 * g + NS, 4, 0:1])
            ins.then_inc(o_sc, 1)
            norm2(3, 4)
            hn2T_copy(2, 2)
            hn2T_copy(3, 4)
            norm2(4, 3)
            hn2T_copy(4, 3)
            act.wait_ge(ex_in, 1)
            A(cand[:, :, 0:NG], cand[:, :, 0:NG], ACT.Exp).then_inc(ex_out, 1)
            act.wait_ge(ex_in, 2)
            A(rs[:, 9, :], rs[:, 9, :], ACT.Exp).then_inc(ex_out, 1)

            act.wait_ge(tbl_rdy, 1)

            def tile_step(s, i, u, first=False, last=False):
                ps, other = (psA, psB)[u], (psA, psB)[1 - u]
                act.wait_ge(gu_ps, s + 1)
                A(sg[64:128, u, :], ps[0:64, 1, :], ACT.Silu).then_inc(sg_rdy, 1)
                if not first:
                    tail(s - 1, i, 1 - u)
                x0 = act.value_load(xb[0:1, bass.ds(s, 1)], min_val=0, max_val=NX)
                x1 = act.value_load(xb[0:1, bass.ds(s + 1, 1)], min_val=0, max_val=NX)
                with act.If(x0 < x1), act.Fori(x0, x1) as x:
                    act.wait_ge(xx_gu, x + 1)
                    A(xsg[64:128], other[0:64, 1, :], ACT.Silu).then_inc(xx_sg, 1)
                    act.wait_ge(xx_hT, x + 1)
                    A(xhT, other[:, 2, 0:256].rearrange("p (k c) -> p k c", k=4), ACT.Copy).then_inc(xx_hTev, 1)
                    act.wait_ge(xx_dn, x + 1)
                    A(xyst[0:C, 0:512], other[0:64, 0, :], ACT.Copy).then_inc(xx_y0, 1)

            def tail(s, n_stored, u):
                ps = (psA, psB)[u]
                act.wait_ge(hT_ps, s + 1)
                A(hT[:, u, :, :], ps[:, 2, 0:256].rearrange("p (k c) -> p k c", k=4), ACT.Copy).then_inc(hT_ev, 1)
                act.wait_ge(dn_ps, s + 1)
                stored(act, n_stored, u)
                A(yst[0:C, u, 0:512], ps[0:64, 3, :], ACT.Copy).then_inc(y0_ev, 1)

            tile_step(0, 0, 0, first=True)
            tile_step(1, 0, 1)
            tile_step(2, 0, 0)
            with act.Fori(1, NE // 2 - 1) as i:
                tile_step(i * 2 + 1, i, 1)
                tile_step(i * 2 + 2, i, 0)
            tile_step(NE - 1, NE // 2 - 1, 1)
            tail(NE - 1, NE // 2 - 1, 1)
            def scale_first(t):
                r = ROWS[t]
                act.wait_ge(y_in[t], 32)
                A(yin[0:r, 2 * t, :], yin[0:r, 2 * t, :], ACT.Copy, scale=cw[0:r, 0, t:t + 1]).then_inc(f_scaled, 1)

            A(fx[:, 0:1], epsc[:, :], ACT.Sqrt)
            scale_first(LAST_ORDER[0])
            scale_first(LAST_ORDER[1])
            for n, t in enumerate(LAST_ORDER):
                if n + 2 < NT:
                    scale_first(LAST_ORDER[n + 2])
                r = ROWS[t]
                act.wait_ge(f_sum, n + 1)
                link(A(yin[0:r, 2 * t, :], x2[0:r, t, :], ACT.Square, accum_out=fx[0:r, t:t + 1]))
                A(ss[0:r, 2, t:t + 1], fx[0:r, t:t + 1], ACT.Sqrt, scale=1.0 / D, bias=epsc[0:r, :]).then_inc(f_rt, 1)

        @block.vector
        def _(dve):
            V = nc.vector
            steps = [0]

            def link(ins):
                steps[0] += 1
                ins.then_inc(dve_step, 1)
                dve.wait_ge(dve_step, steps[0])

            def tt(out, x, y, op):
                return V.tensor_tensor(out, x, y, op)

            V.memset(epsc[:, :], EPS)
            V.memset(st[:, :], 1.0).then_inc(ms_rdy, 1)
            V.memset(rab[:, :, :], 1.0)
            link(V.memset(ss[:, :, :], 1.0))

            def scale_x(t):
                r = ROWS[t]
                dve.wait_ge(rms_rdy, t + 1)
                link(V.reciprocal(st[0:r, 16 + t:17 + t], st[0:r, 8 + t:9 + t]))
                V.tensor_scalar(xrow(t), xrow(t), st[0:r, 16 + t:17 + t], None, ALU.mult).then_inc(x_scaled, 1)

            def hnT_copy(t):
                dve.wait_ge(xT_ps, t + 1)
                r = ROWS[t]
                for j in range(2 if t < 4 else 1):
                    nk = 4 if t < 4 else 8
                    src = psA[:, 2 * (t % 2) + j, 0:nk * r].rearrange("p (k n) -> p k n", k=nk)
                    gain = g1[:, 4 * j:4 * j + nk].unsqueeze(2).to_broadcast([128, nk, r])
                    ins = tt(hnT[:, 4 * j:4 * j + nk, t * 128:t * 128 + r], src, gain, ALU.mult)
                ins.then_inc(hn_copied, 1)

            scale_x(0)
            scale_x(1)
            dve.wait_ge(g1_in, 16)
            for t in range(NT):
                hnT_copy(t)
                if t + 2 < NT:
                    scale_x(t + 2)
                if t == 1:
                    dve.wait_ge(lam_in, 48)
                    link(V.tensor_copy(lraw[32:48, :].rearrange("q (g s) -> q g s", g=2),
                                       ldt[32:48, :].unsqueeze(2).to_broadcast([NQ, 2, 64])))
                    V.memset(Lp[:, 0, :, 0:1], 1.0).then_inc(lraw_rdy, 1)
                    V.memset(Lp[:, 1, :, 0:1], 0.0)

            dve.wait_ge(lam_ps, 1)
            V.tensor_copy(lT[:, :, :], psB[:, 3, 0:48].rearrange("p (a q) -> p a q", a=3)).then_inc(small_ev, 1)

            lr, li, dt = lT[:, 0, :], lT[:, 1, :], lT[:, 2, :]
            c = [sc[:, j, :] for j in range(16)]
            dve.wait_ge(pre_a, 1)
            tt(c[0], lr, dt, ALU.mult)
            link(tt(c[6], li, dt, ALU.mult))
            link(V.tensor_scalar(c[7], c[6], 1.0 / TWO_PI, MAGIC, ALU.mult, ALU.add))
            link(V.tensor_scalar(c[7], c[7], -MAGIC, None, ALU.add))
            for part in (PI2_A, PI2_B, PI2_C):
                link(V.scalar_tensor_tensor(c[6], c[7], -part, c[6], ALU.mult, ALU.add))
            V.tensor_scalar(c[2], c[6], 3.1415925, -3.1415925, ALU.min, ALU.max).then_inc(pre_v, 1)
            dve.wait_ge(pre_a, 5)
            link(tt(c[7], c[5], c[5], ALU.mult))
            link(V.tensor_scalar(c[7], c[7], -2.0, 1.0, ALU.mult, ALU.add))
            cos1, sin1 = c[7], c[4]
            tt(Lp[:, 0, :, 1], c[1], cos1, ALU.mult)
            link(tt(Lp[:, 1, :, 1], c[1], sin1, ALU.mult))

            def cmul(o_r, o_i, a_r, a_i, b_r, b_i, t1, t2):
                link(tt(t1, a_i, b_i, ALU.mult))
                link(tt(t2, a_r, b_r, ALU.mult))
                link(tt(o_r, t2, t1, ALU.subtract))
                link(tt(t1, a_r, b_i, ALU.mult))
                link(tt(t2, a_i, b_r, ALU.mult))
                link(tt(o_i, t1, t2, ALU.add))

            P = lambda r, e: Lp[:, r, :, e]
            cmul(P(0, 2), P(1, 2), P(0, 1), P(1, 1), P(0, 1), P(1, 1), c[8], c[9])
            cmul(P(0, 3), P(1, 3), P(0, 2), P(1, 2), P(0, 1), P(1, 1), c[8], c[9])
            cmul(P(0, 4), P(1, 4), P(0, 2), P(1, 2), P(0, 2), P(1, 2), c[8], c[9])
            cmul(c[10], c[11], cos1, sin1, cos1, sin1, c[8], c[9])
            cmul(rot[:, 0, :, 1], rot[:, 1, :, 1], c[10], c[11], c[10], c[11], c[8], c[9])
            link(V.memset(rot[:, 0, :, 0:1], 1.0))
            V.memset(rot[:, 1, :, 0:1], 0.0).then_inc(lp_rdy, 1)
            link(tt(c[8], lr, lr, ALU.mult))
            link(tt(c[9], li, li, ALU.mult))
            link(tt(c[8], c[8], c[9], ALU.add))
            link(V.reciprocal(c[12], c[8]))
            link(V.tensor_scalar(c[13], P(0, 1), -1.0, None, ALU.add))
            link(tt(c[8], c[13], lr, ALU.mult))
            link(tt(c[9], P(1, 1), li, ALU.mult))
            link(tt(c[8], c[8], c[9], ALU.add))
            link(tt(c[14], c[8], c[12], ALU.mult))
            link(tt(c[8], P(1, 1), lr, ALU.mult))
            link(tt(c[9], c[13], li, ALU.mult))
            link(tt(c[8], c[8], c[9], ALU.subtract))
            link(tt(c[15], c[8], c[12], ALU.mult))
            dve.wait_ge(bc_in, 32)
            k_r = c[14].unsqueeze(2).to_broadcast([128, NQ, 16])
            k_i = c[15].unsqueeze(2).to_broadcast([128, NQ, 16])
            b1 = prod1[:, :, 0, :]
            b2 = prod1[:, :, 1, :]
            cmul(Bc[:, 0], Bc[:, 1], k_r, k_i, Bb[:, 0], Bb[:, 1], b1, b2)
            dve.wait_ge(small_ps, 1)
            for r in range(2):
                for par in range(2):
                    src = psA[:, 2 + r, :].rearrange("p (q g h) -> p g q h", g=2, h=16)[64 * par:64 * par + 64, par]
                    V.tensor_copy(CT[64 * par:64 * par + 64, r], src)
            V.tensor_copy(WT[:, :, :].rearrange("p h i -> p (h i)"), psA[:, 1, :])
            V.tensor_copy(h0T[:, :, :, :].rearrange("p r n q -> p (r n q)"), psA[:, 0, 0:256]).then_inc(small_ev, 1)
            dve.wait_ge(consts, 2)
            dve.wait_ge(xT_ps, NT)
            Lb = lambda r: Lp[:, r, :, 0:T].unsqueeze(3).to_broadcast([128, NQ, T, 16])
            Bx = lambda r: Bc[:, r].unsqueeze(2).to_broadcast([128, NQ, T, 16])
            for r in range(2):
                link(tt(prod1, Lb(0), Bx(r), ALU.mult))
                link(tt(prod2, Lb(1), Bx(1 - r), ALU.mult))
                for g in range(2):
                    h = slice(64 * g, 64 * g + 64)
                    ins = tt(PTst[h, :, r, :, 16 * g:16 * g + 16], prod1[h], prod2[h],
                             ALU.subtract if r == 0 else ALU.add)
                if r == 0:
                    link(ins)
            ins.then_inc(ptst_rdy, 1)
            dve.wait_ge(ptst_rdy, 1)

            dve.wait_ge(xa_ps, 4)
            for e in range(T):
                for ql in range(2, 4):
                    ins = V.tensor_copy(*u_copy(ql, e))
            ins.then_inc(u_copied, 1)
            dve.wait_ge(u_zero, 1)
            dve.wait_ge(zT_ps, 1)
            for e, at in ((3, NB), (0, NB + NS)):
                for ql in range(4):
                    src = psA[32 * ql:32 * ql + 32, 1, 0:32].rearrange("p (m n) -> p m n", m=4)
                    dst = U[32 * e:32 * e + 32, :, at:at + NS].rearrange("p (m l) n -> p l m n", l=4)[:, ql]
                    ins = V.tensor_copy(dst, src)
            ins.then_inc(zT_used, 1)

            dve.wait_ge(misc_in, 16 * 7)
            link(tt(Dd_all, ident[0:32, 0:32].unsqueeze(1).to_broadcast([32, NQ, 32]),
                    Dc[:, :].unsqueeze(2).to_broadcast([32, NQ, 32]), ALU.mult))
            Mps = psB[0:32, :, :].rearrange("p a (b n) -> p (a b) n", n=128)
            dve.wait_ge(m_ps, 1)
            for e in range(T):
                blk = 32 * (3 - e)
                link(tt(MT[32 * e:32 * e + 32, :, blk:blk + 32], Mps[:, :, 0:32], Dd_all, ALU.add))
                if e:
                    ins = V.tensor_copy(MT[32 * e:32 * e + 32, :, blk + 32:128], Mps[:, :, 32:32 * (e + 1)])
                    if e < T - 1:
                        link(ins)
            ins.then_inc(m_copied, 1)

            q8 = lambda ap, h: ap[:, 8 * h:8 * h + 8]
            S = lambda j: T4[:, j, :].rearrange("p (q b) -> p q b", q=8)
            for h in range(2):
                cosb, sinb = q8(rot[:, 0], h), q8(rot[:, 1], h)
                Vr, Vi = q8(VH[:, 0], h)[:, :, 0:NB], q8(VH[:, 1], h)[:, :, 0:NB]
                dve.wait_ge(rot_rdy, 1)
                dec = decay.rearrange("p (q b) -> p q b", q=8)
                link(V.tensor_copy(dec, c[3][:, 8 * h:8 * h + 8].unsqueeze(2).to_broadcast([128, 8, NB])))
                link(V.memset(dec[:, :, 0:1], 0.0))
                dve.wait_ge(v_copied, 4 * (h + 1))
                link(tt(S(0), Vr, cosb, ALU.mult))
                link(tt(S(1), Vi, sinb, ALU.mult))
                link(tt(S(0), S(0), S(1), ALU.add))
                link(V.tensor_tensor_scan(T4[:, 1, :], decay, T4[:, 0, :], 0.0, ALU.mult, ALU.add))
                dve.wait_ge(turned_im, h + 1)
                link(V.tensor_tensor_scan(T4[:, 3, :], decay, T4[:, 2, :], 0.0, ALU.mult, ALU.add))
                Hr, Hi = q8(VH[:, 0], h), q8(VH[:, 1], h)
                for r, (H, x, y, op) in enumerate(((Hr, cosb, sinb, ALU.subtract), (Hi, sinb, cosb, ALU.add))):
                    link(tt(S(0), S(1), x, ALU.mult))
                    link(tt(S(2), S(3), y, ALU.mult))
                    tt(H[:, :, 1:NB], S(0)[:, :, 0:NB - 1], S(2)[:, :, 0:NB - 1], op)
                    link(tt(hfin[:, r, 8 * h:8 * h + 8], S(0)[:, :, NB - 1], S(2)[:, :, NB - 1], op))
                    V.memset(H[:, :, 0:1], 0.0)
                    ins = V.tensor_copy(H[:, :, NB:NB + NS], h0T[:, r].rearrange("p n q -> p q n")[:, 8 * h:8 * h + 8])
                    if r == 0 or h == 1:
                        link(ins)
                if h == 1:
                    L1 = lambda r: Lp[:, r, :, 1].unsqueeze(1).to_broadcast([128, NS, NQ])
                    s1 = T4[:, 0, 0:128].rearrange("p (n q) -> p n q", n=NS)
                    s2 = T4[:, 1, 0:128].rearrange("p (n q) -> p n q", n=NS)
                    cmul(hnew[:, 0], hnew[:, 1], L1(0), L1(1), h0T[:, 0], h0T[:, 1], s1, s2)
                    for r in range(2):
                        ins = tt(hnew[:, r], hnew[:, r], VH[:, r, :, NB + NS:UC].rearrange("p q n -> p n q"), ALU.add)
                ins.then_inc(h_rdy, 1)

            heads = lambda ap: ap.rearrange("p (h n) -> p h n", h=NH)
            v_tiles = [vb[:, t, :] for t in range(4)] + [vbs[0:NS]]
            for t in range(NT):
                r = ROWS[t]
                if t < 4:
                    dve.wait_ge(in_ev, 5 + t)
                else:
                    dve.wait_ge(zT_used, 3)
                scr = decay[0:r, 512 * (t % 2):512 * (t % 2) + DS]
                link(tt(scr, v_tiles[t], v_tiles[t], ALU.mult))
                V.tensor_reduce(st[0:r, 24 + 4 * t:28 + 4 * t], heads(scr), AX.X, ALU.add)
                link(tt(v_tiles[t], v_tiles[t], gmg[0:r], ALU.mult))
            V.tensor_scalar(st[:, 24:44], st[:, 24:44], 1.0 / 128, EPS, ALU.mult, ALU.add).then_inc(gq, 1)
            dve.wait_ge(gr, 1)
            link(V.reciprocal(st[:, 44:64], st[:, 24:44]))
            for t in range(NT):
                r = ROWS[t]
                tt(heads(v_tiles[t]), heads(v_tiles[t]), st[0:r, 44 + 4 * t:48 + 4 * t].unsqueeze(2).to_broadcast([r, NH, 128]),
                   ALU.mult).then_inc(vbn, 1)
            dve.wait_ge(hout_ps, 1)
            V.tensor_copy(hout[0:32, 0, :], psA[0:32, 0, 0:128])
            V.tensor_copy(hout[:, 1:3, :], psA[:, 0, 128:384].rearrange("p (r s) -> p r s", r=2))
            link(tt(vsT, psA[:, 0, 384:416].rearrange("p (h n) -> p h n", h=4), w00[:, :, 0:1].to_broadcast([128, NH, NS]), ALU.mult))
            tt(vsT, vsT, w00[:, :, 1:2].to_broadcast([128, NH, NS]), ALU.add).then_inc(hout_copied, 1)

            dve.wait_ge(y_ev, 4)
            dve.wait_ge(zT_used, 4)
            for m in range(4):
                link(tt(sigT[:, m, :], mixT[:, m, :], sigT[:, m, :], ALU.mult))
                V.tensor_scalar(mixT[:, m, :], sigT[:, m, :], gab[:, m:m + 1], None, ALU.mult).then_inc(ya_rdy, 1)
            for h in range(NH):
                yb, ub = mixT[:, 4 + h, 0:NP_], uT[:, h, 0:NP_]
                dve.wait_ge(s_ps, h + 1)
                link(tt(yb.rearrange("p (c i) -> p c i", c=4), psA[:, h, :].rearrange("p (c i) -> p c i", c=4),
                        bsb[:, h, :].unsqueeze(1).to_broadcast([128, 4, 128]), ALU.add))
                link(tt(ub, yb, ub, ALU.mult))
                V.tensor_scalar(yb, ub, gab[:, 4 + h:5 + h], None, ALU.mult).then_inc(yb_rdy, 1)
            ubs = uT[:, :, NP_:NTOK]
            link(tt(ubs, vsT, ubs, ALU.mult))
            tt(mixT[:, 4:8, NP_:NTOK], ubs, gab[:, 4:8].unsqueeze(2).to_broadcast([128, NH, NS]), ALU.mult).then_inc(yb_rdy, 1)
            dve.wait_ge(rab_ps, 1)
            for j in range(2):
                V.tensor_copy(rab[:, 0:4, j], psA[:, 1 - j, 64:68])
            for g in range(4):
                ins = V.tensor_copy(rab[32 * g:32 * g + NS, 4, 0:1], psA[32 * g:32 * g + NS, 1 if g < 2 else 0, 68:69])
            link(ins)
            V.tensor_scalar(rab[:, :, :], rab[:, :, :], 1.0 / DS, EPS, ALU.mult, ALU.add).then_inc(rab_ms, 1)
            dve.wait_ge(rab_rt, 1)
            link(V.reciprocal(rab[:, :, :], rab[:, :, :]))
            dve.wait_ge(rest_in, 16 * 6)
            V.memset(LG, 0.0)

            def normed(n, t):
                r = ROWS[t]
                dve.wait_ge(n2rt, n + 1)
                link(V.reciprocal(ss[0:r, 3, t:t + 1], ss[0:r, 1, t:t + 1]))
                V.scalar_tensor_tensor(hn2[0:r, n % 2, :], x2[0:r, t, :], ss[0:r, 3, t:t + 1], g2b[0:r],
                                       ALU.mult, ALU.mult).then_inc(hn2_rdy, 1)

            def logits(n, t):
                r = ROWS[t]
                dve.wait_ge(lg_ps, n + 1)
                tt(LG[0:r, t, :], (psB, psA)[t % 2][0:r, 2, 0:36], brb[0:r], ALU.add).then_inc(lg_ev, 1)

            for n, t in enumerate(ORDER):
                ps = (psB, psA)[t % 2]
                if t < 4:
                    dve.wait_ge(o_ps, n + 1)
                    dve.wait_ge(x_in[t], 32)
                    for j in range(2):
                        for h in range(2):
                            xh = x2[:, t, 512 * h:512 * h + 512]
                            ins = V.scalar_tensor_tensor(xh, ps[:, 2 * j + h, :], rab[:, t, j:j + 1], xh, ALU.mult, ALU.add)
                            if j == 0:
                                link(ins)
                else:
                    dve.wait_ge(o_sc, 1)
                    dve.wait_ge(x_in[4], 32)
                    x2s = x2[0:NS, 4, :].rearrange("p (h n) -> p h n", h=2)
                    link(tt(x2s, x2s, tsm[:, 0:2, :], ALU.add))
                    ins = tt(x2s, x2s, tsm[:, 2:4, :], ALU.add)
                ins.then_inc(o_ev, 1)
                normed(n, t)
                if n:
                    logits(n - 1, ORDER[n - 1])
            logits(NT - 1, ORDER[NT - 1])

            R = lambda j: rs[:, j, :]
            def b(ap, n):
                return ap.unsqueeze(2).to_broadcast([128, NT, n])

            iota = iof.unsqueeze(1)

            def first_max(x, m, oh, n, scr):
                link(V.tensor_reduce(m, x, AX.X, ALU.max))
                link(tt(scr, x, b(m, n), ALU.is_ge))
                link(V.scalar_tensor_tensor(scr, scr, -1000.0, iota[:, :, 0:n].to_broadcast([128, NT, n]), ALU.mult, ALU.add))
                link(V.tensor_reduce(R(15), scr, AX.X, ALU.min))
                link(tt(oh, scr, b(R(15), n), ALU.is_equal))

            gl, el = LG[:, :, 0:NG], LG[:, :, NG:]
            ohg = oh1[:, :, 0:NG]
            dve.wait_ge(lg_ev, NT)
            dve.wait_ge(iota_rdy, 1)
            first_max(gl, R(0), ohg, NG, eqb[:, :, 0:NG])
            tt(cand[:, :, 0:NG], gl, b(R(0), NG), ALU.subtract).then_inc(ex_in, 1)
            dve.wait_ge(ex_out, 1)
            link(V.tensor_reduce(R(1), cand[:, :, 0:NG], AX.X, ALU.add))
            link(V.reciprocal(R(2), R(1)))
            link(V.tensor_scalar(eqb[:, :, 0:NG], ohg, -1.0, BIG, ALU.add, ALU.mult))
            link(tt(el2.rearrange("p t (g e) -> p t g e", g=NG), el.rearrange("p t (g e) -> p t g e", g=NG),
                    eqb[:, :, 0:NG].unsqueeze(3).to_broadcast([128, NT, NG, EPG]), ALU.add))
            first_max(el2, R(3), oh1, NE, cand)
            link(V.scalar_tensor_tensor(el2, oh1, -2.0 * BIG, el2, ALU.mult, ALU.add))
            first_max(el2, R(4), oh2, NE, cand)
            tt(R(9), R(4), R(3), ALU.subtract).then_inc(ex_in, 1)
            link(tt(eqb, oh1, oh2, ALU.add))
            V.tensor_copy(ohb[:, :, :], eqb).then_inc(oh_rdy, 1)
            dve.wait_ge(ex_out, 2)
            link(V.tensor_scalar(R(10), R(9), 1.0, None, ALU.add))
            link(V.reciprocal(R(10), R(10)))
            link(tt(cw[:, 0, :], R(10), R(2), ALU.mult))
            link(tt(cw[:, 1, :], cw[:, 0, :], R(9), ALU.mult))
            both = [128, 2 * NT, NE]
            W = lambda j: rs12[:, j, :]
            link(tt(prod12, oh12, iota.to_broadcast(both), ALU.mult))
            link(V.tensor_reduce(W(0), prod12, AX.X, ALU.add))
            ones_row, xt, xs, d = (eqb[:, m, :] for m in range(4))
            link(V.memset(ones_row, 1.0))
            dve.wait_ge(pre_ps, 1)
            link(tt(prod12.rearrange("p (j t) e -> p j (t e)", j=2), oh12.rearrange("p (j t) e -> p j (t e)", j=2),
                    psA[:, 0, 0:NT * NE].unsqueeze(1).to_broadcast([128, 2, NT * NE]), ALU.mult))
            link(V.tensor_reduce(W(1), prod12, AX.X, ALU.add))
            link(V.tensor_scalar(xt, psA[:, 1, 0:NE], 1.0 / C, -(C / 2 + 0.5) / C, ALU.mult, ALU.add))
            link(V.tensor_scalar(xt, xt, MAGIC, None, ALU.add))
            link(V.tensor_scalar(xt, xt, -MAGIC, 0.0, ALU.add, ALU.max))
            link(V.tensor_tensor_scan(xs, ones_row, xt, 0.0, ALU.mult, ALU.add))
            V.memset(xb[0:1, 0:1], 0)
            V.tensor_copy(xb[0:1, 1:NE + 1], xs[0:1])
            link(tt(d, xs, xt, ALU.subtract))
            link(tt(d, d, iof, ALU.subtract))
            link(tt(prod12, oh12, d.unsqueeze(1).to_broadcast(both), ALU.mult))
            link(V.tensor_reduce(W(2), prod12, AX.X, ALU.add))
            link(V.tensor_scalar(W(3), W(1), 1.0 / C, -(C / 2 - 0.5) / C, ALU.mult, ALU.add))
            link(V.tensor_scalar(W(3), W(3), MAGIC, None, ALU.add))
            link(V.tensor_scalar(W(3), W(3), -MAGIC, None, ALU.add))
            link(V.scalar_tensor_tensor(W(4), W(3), float(-C), W(1), ALU.mult, ALU.add))
            link(V.scalar_tensor_tensor(W(5), W(2), float(NE - 1), W(3), ALU.add, ALU.add))
            link(V.scalar_tensor_tensor(W(5), W(3), 1.0, W(5), ALU.min, ALU.mult))
            link(tt(W(5), W(5), W(0), ALU.add))
            dve.wait_ge(vals_rdy, 1)
            tt(row_oh, iot.unsqueeze(1).to_broadcast([128, 2 * NT, C]), W(4).unsqueeze(2).to_broadcast([128, 2 * NT, C]), ALU.is_equal)
            link(tt(tile_oh, iot[:, 0:NTL].unsqueeze(1).to_broadcast([128, 2 * NT, NTL]),
                    W(5).unsqueeze(2).to_broadcast([128, 2 * NT, NTL]), ALU.is_equal))
            for w in range(2):
                ins = tt(entry[:, :, :, w], tile_oh, vals.rearrange("p j t w -> p (j t) w")[:, :, w:w + 1].to_broadcast([128, 2 * NT, NTL]), ALU.mult)
            ins.then_inc(slot_rdy, 1)
            dve.wait_ge(tbl_ps, 1)
            V.tensor_scalar(tbl.rearrange("c t w -> c (t w)"), psA[0:C, 2, 0:2 * NTL], float(INVALID), None, ALU.add).then_inc(tbl_rdy, 1)

            def xT_copy(s, u):
                dve.wait_ge(xgT_ps, s + 1)
                V.tensor_copy(xgT[:, u].rearrange("p k c -> p (k c)"), (psA, psB)[u][:, 0, :]).then_inc(xgT_ev, 1)

            def tail(s, n_stored, u):
                dve.wait_ge(dn_ps, s + 1)
                stored(dve, n_stored, u)
                V.tensor_copy(yst[0:C, u, 512:1024], (psA, psB)[u][64:128, 3, :]).then_inc(y1_ev, 1)

            def tile_step(s, i, u, first=False, last=False):
                ps, other = (psA, psB)[u], (psA, psB)[1 - u]
                dve.wait_ge(sg_rdy, s + 1)
                V.tensor_tensor(hh[0:64, u, :], sg[64:128, u, :], ps[64:128, 1, :], ALU.mult).then_inc(h_done, 1)
                if not last:
                    xT_copy(s + 1, 1 - u)
                if not first:
                    tail(s - 1, i, 1 - u)
                x0 = dve.value_load(xb[0:1, bass.ds(s, 1)], min_val=0, max_val=NX)
                x1 = dve.value_load(xb[0:1, bass.ds(s + 1, 1)], min_val=0, max_val=NX)
                with dve.If(x0 < x1), dve.Fori(x0, x1) as x:
                    dve.wait_ge(xx_T, x + 1)
                    V.tensor_copy(xxgT.rearrange("p k c -> p (k c)"), ps[:, 0, :]).then_inc(xx_Tev, 1)
                    dve.wait_ge(xx_sg, x + 1)
                    V.tensor_tensor(xhh[0:64], xsg[64:128], other[64:128, 1, :], ALU.mult).then_inc(xx_h, 1)
                    dve.wait_ge(xx_dn, x + 1)
                    V.tensor_copy(xyst[0:C, 512:1024], other[64:128, 0, :]).then_inc(xx_y1, 1)

            xT_copy(0, 0)
            tile_step(0, 0, 0, first=True)
            tile_step(1, 0, 1)
            tile_step(2, 0, 0)
            with dve.Fori(1, NE // 2 - 1) as i:
                tile_step(i * 2 + 1, i, 1)
                tile_step(i * 2 + 2, i, 0)
            tile_step(NE - 1, NE // 2 - 1, 1, last=True)
            tail(NE - 1, NE // 2 - 1, 1)

            def add_second(n):
                t = LAST_ORDER[n]
                r = ROWS[t]
                dve.wait_ge(y_in[t], 32)
                dve.wait_ge(f_first, n + 1)
                V.scalar_tensor_tensor(x2[0:r, t, :], yin[0:r, 2 * t + 1, :], cw[0:r, 1, t:t + 1], x2[0:r, t, :],
                                       ALU.mult, ALU.add).then_inc(f_sum, 1)

            add_second(0)
            for n, t in enumerate(LAST_ORDER):
                if n + 1 < NT:
                    add_second(n + 1)
                r = ROWS[t]
                dve.wait_ge(f_rt, n + 1)
                link(V.reciprocal(ss[0:r, 3, t:t + 1], ss[0:r, 2, t:t + 1]))
                V.scalar_tensor_tensor(x2[0:r, t, :], x2[0:r, t, :], ss[0:r, 3, t:t + 1], gfb[0:r],
                                       ALU.mult, ALU.mult).then_inc(f_done, 1)

        @block.gpsimd
        def _(pool):
            G = nc.gpsimd
            steps = [0]

            def link(ins):
                steps[0] += 1
                ins.then_inc(pool_step, 1)
                pool.wait_ge(pool_step, steps[0])

            def tt(out, x, y, op):
                return G.tensor_tensor(out, x, y, op)

            link(G.memset(ident[:, :], 0.0))
            link(G.affine_select(out=ident[:, :], in_=ident[:, :], compare_op=ALU.not_equal, fill=1.0, base=0,
                                 pattern=[[-1, 128]], channel_multiplier=1))
            G.memset(ones[:, :], 1.0)
            link(G.memset(sel[:, :], 0.0))
            for j in range(4):
                ins = G.tensor_copy(sel[32 * j:32 * j + NS, :], ident[32 * j:32 * j + NS, 32 * j:32 * j + NS])
            link(ins)
            G.memset(trib[:, :], 1.0).then_inc(consts, 1)
            link(G.memset(PTst, 0.0))
            link(G.memset(QT, 0.0))
            G.memset(MT, 0.0).then_inc(consts, 1)
            G.memset(U[:, :, NB:UC], 0.0).then_inc(u_zero, 1)
            pool.wait_ge(ws_in, 16)
            G.affine_select(out=Ws, in_=Ws, compare_op=ALU.is_ge, fill=0.0, base=0,
                            pattern=[[0, NH], [-1, 128]], channel_multiplier=1).then_inc(ws_masked, 1)
            G.memset(oneb[:, :], 1.0)
            G.affine_select(out=trib[:, :], in_=trib[:, :], compare_op=ALU.is_gt, fill=0.0, base=0,
                            pattern=[[1, 128]], channel_multiplier=-1)
            G.iota(iof, [[1, 32]], base=0, channel_multiplier=0, allow_small_or_imprecise_dtypes=True).then_inc(iota_rdy, 1)
            pool.wait_ge(xT_ps, NT)
            G.memset(zs, 0.0).then_inc(zs_zero, 1)

            pool.wait_ge(lp_rdy, 1)
            pool.wait_ge(small_ev, 2)
            Lb = lambda r: Lp[:, r].unsqueeze(3).to_broadcast([128, NQ, 5, 16])
            Cx = lambda r: CT[:, r].unsqueeze(2).to_broadcast([128, NQ, 5, 16])
            QTe = QT.rearrange("p q r (e n) -> p q r e n", e=5)
            for r in range(2):
                if r:
                    link(G.tensor_scalar(CT[:, 1], CT[:, 1], -1.0, None, ALU.mult))
                link(tt(prodq1, Lb(0), Cx(r), ALU.mult))
                link(tt(prodq2, Lb(1), Cx(1 - r), ALU.mult))
                for g in range(2):
                    h = slice(64 * g, 64 * g + 64)
                    ins = tt(QTe[h, :, r, :, 16 * g:16 * g + 16], prodq1[h], prodq2[h], ALU.subtract)
                if r == 0:
                    link(ins)
            ins.then_inc(qt_rdy, 1)
            pool.wait_ge(qt_rdy, 1)

            m_r, m_i = T4[:, 2, 0:NQ], T4[:, 2, NQ:2 * NQ]
            s1, s2 = T4[:, 2, 2 * NQ:3 * NQ], T4[:, 2, 3 * NQ:4 * NQ]

            def cmul(o_r, o_i, a_r, a_i, b_r, b_i, t1, t2):
                link(tt(t1, a_i, b_i, ALU.mult))
                link(tt(t2, a_r, b_r, ALU.mult))
                link(tt(o_r, t2, t1, ALU.subtract))
                link(tt(t1, a_r, b_i, ALU.mult))
                link(tt(t2, a_i, b_r, ALU.mult))
                return tt(o_i, t1, t2, ALU.add)

            w = 2
            while w < NB:
                link(cmul(m_r, m_i, rot[:, 0, :, w - 1], rot[:, 1, :, w - 1], rot[:, 0, :, 1], rot[:, 1, :, 1], s1, s2))
                t1 = T4[:, 0, 0:NQ * w].rearrange("p (q b) -> p q b", q=NQ)
                t2 = T4[:, 1, 0:NQ * w].rearrange("p (q b) -> p q b", q=NQ)
                ins = cmul(rot[:, 0, :, w:2 * w], rot[:, 1, :, w:2 * w], rot[:, 0, :, 0:w], rot[:, 1, :, 0:w],
                           m_r.unsqueeze(2).to_broadcast([128, NQ, w]), m_i.unsqueeze(2).to_broadcast([128, NQ, w]), t1, t2)
                w *= 2
                if w < NB:
                    link(ins)
            ins.then_inc(rot_rdy, 1)
            pool.wait_ge(rot_rdy, 1)

            for h in range(2):
                q8 = lambda ap: ap[:, 8 * h:8 * h + 8]
                S = lambda j: T4[:, j, :].rearrange("p (q b) -> p q b", q=8)
                pool.wait_ge(v_copied, 4 * (h + 1))
                if h:
                    pool.wait_ge(h_rdy, 1)
                link(tt(S(2), q8(VH[:, 1])[:, :, 0:NB], q8(rot[:, 0]), ALU.mult))
                link(tt(S(3), q8(VH[:, 0])[:, :, 0:NB], q8(rot[:, 1]), ALU.mult))
                tt(S(2), S(2), S(3), ALU.subtract).then_inc(turned_im, 1)

            pool.wait_ge(h_rdy, 2)
            G.iota(iot, [[1, C]], base=0, channel_multiplier=0, allow_small_or_imprecise_dtypes=True)
            for j in range(2):
                for w in range(2):
                    ins = G.iota(vals[:, j, :, w], [[128, NT]], base=w * j * NTOK - INVALID, channel_multiplier=1,
                                 allow_small_or_imprecise_dtypes=True)
            ins.then_inc(vals_rdy, 1)

            pool.wait_ge(tbl_rdy, 1)
            pool.wait_ge(hn2_out[0], 48)
            pool.wait_ge(hn2_out[1], 32)

            def gather(dst, rows_ap):
                return G.indirect_dma_start(out=dst, out_offset=None, in_=hn2_d[:, :],
                                            in_offset=bass.IndirectOffsetOnAxis(ap=rows_ap, axis=0),
                                            bounds_check=NTOK - 1, oob_is_err=False)

            def scatter(src, rows_ap):
                return G.indirect_dma_start(out=y2_d[:, :], out_offset=bass.IndirectOffsetOnAxis(ap=rows_ap, axis=0),
                                            in_=src, in_offset=None, bounds_check=2 * NTOK - 1, oob_is_err=False)

            def wait_before(signal, count):
                count = count if isinstance(count, int) else pool.to_reg(count)
                pool.wait_ge(tbl_rdy, 1)
                pool.wait_ge(signal, count)

            def fetch(s, u):
                G.tensor_copy(ig[:, u:u + 1], tbl[:, bass.ds(s, 1), 0]).then_inc(ig_rdy, 1)
                wait_before(ig_rdy, s + 1)
                gather(xg[0:C, u, :], ig[:, u:u + 1]).then_inc(xg_in[u], 16)

            def store(s, n_stored, u):
                stored(pool, n_stored, u)
                G.tensor_copy(isc[:, u:u + 1], tbl[:, bass.ds(s, 1), 1]).then_inc(is_rdy, 1)
                wait_before(y0_ev, s + 1)
                pool.wait_ge(y1_ev, s + 1)
                pool.wait_ge(is_rdy, s + 1)
                scatter(yst[0:C, u, :], isc[:, u:u + 1]).then_inc(y_out[u], 16)

            def fetch_further(x):
                G.tensor_copy(igx[:, :], tbl[:, bass.ds(x + NE, 1), :].rearrange("c t w -> c (t w)")).then_inc(xx_ig, 1)
                wait_before(xx_ig, x + 1)
                gather(xxg[0:C, :], igx[:, 0:1]).then_inc(xx_in, 16)

            def tile_step(s, i, u, first=False, last=False, ahead=True):
                if ahead:
                    pool.wait_ge(xgT_ps, s + 1)
                    fetch(s + 2, u)
                if not first:
                    store(s - 1, i, 1 - u)
                x0 = pool.value_load(xb[0:1, bass.ds(s, 1)], min_val=0, max_val=NX)
                x1 = pool.value_load(xb[0:1, bass.ds(s + 1, 1)], min_val=0, max_val=NX)
                with pool.If(x0 < x1), pool.Fori(x0, x1) as x:
                    wait_before(xx_y0, x + 1)
                    pool.wait_ge(xx_y1, x + 1)
                    scatter(xyst[0:C, :], igx[:, 1:2]).then_inc(xx_out, 16)
                    wait_before(xx_out, (x + 1) * 16)
                    with pool.If(x + 1 < x1):
                        fetch_further(x + 1)
                if not last:
                    x_next = pool.value_load(xb[0:1, bass.ds(s + 2, 1)], min_val=0, max_val=NX)
                    with pool.If(x1 < x_next):
                        fetch_further(x1)

            fetch(0, 0)
            fetch(1, 1)
            x_first = pool.value_load(xb[0:1, 1:2], min_val=0, max_val=NX)
            with pool.If(x_first > 0):
                fetch_further(0)
            tile_step(0, 0, 0, first=True)
            tile_step(1, 0, 1)
            tile_step(2, 0, 0)
            with pool.Fori(1, NE // 2 - 2) as i:
                tile_step(i * 2 + 1, i, 1)
                tile_step(i * 2 + 2, i, 0)
            tile_step(NE - 3, NE // 2 - 2, 1)
            tile_step(NE - 2, NE // 2 - 2, 0, ahead=False)
            tile_step(NE - 1, NE // 2 - 1, 1, last=True, ahead=False)
            store(NE - 1, NE // 2 - 1, 1)
            for n, t in enumerate(LAST_ORDER):
                r = ROWS[t]
                pool.wait_ge(f_scaled, n + 1)
                tt(x2[0:r, t, :], x2[0:r, t, :], yin[0:r, 2 * t, :], ALU.add).then_inc(f_first, 1)

        @block.tensor
        def _(pe):
            def mm(out, lhsT, rhs, start, stop):
                return nc.tensor.matmul(out, lhsT, rhs, start=start, stop=stop, skip_group_check=True)

            def tr(out, in_):
                p = in_.shape[0]
                b0 = in_.base_partition() if callable(in_.base_partition) else in_.base_partition
                return nc.tensor.transpose(out, in_, ident[b0:b0 + p, b0:b0 + p])

            pe.wait_ge(consts, 1)
            for t in range(NT):
                r = ROWS[t]
                pe.wait_ge(x_scaled, t + 1)
                if t >= 2:
                    pe.wait_ge(hn_copied, t - 1)
                cols = xrow(t).rearrange("p (m k) -> p k m", k=KD)
                for k in range(KD):
                    if t < 4:
                        out = psA[:, 2 * (t % 2) + k // 4, 128 * (k % 4):128 * (k % 4) + 128]
                    else:
                        out = psA[:, 0, NS * k:NS * k + NS]
                    ins = tr(out, cols[:, k])
                ins.then_inc(xT_ps, 1)
            pe.wait_ge(lraw_rdy, 1)
            tr(psB[:, 3, 0:48], lraw).then_inc(lam_ps, 1)
            pe.wait_ge(hn_copied, NT)

            def partial(w):
                for k in range(KD):
                    j = k % 4
                    ins = mm(psA[32 * j:32 * j + NS, 0, :], hnT[:, k, NP_:NTOK], w[:, k, :], k < 4, k >= 4)
                ins.then_inc(zp_ps, 1)

            def total_T(r):
                pe.wait_ge(zs_copied, r + 1)
                if r:
                    pe.wait_ge(zT_used, r)
                for m in range(4):
                    ins = mm(psA[:, 1, NS * m:NS * m + NS], zs[:, 128 * m:128 * m + 128], sel[:, :], True, True)
                ins.then_inc(zT_ps, 1)

            pe.wait_ge(w_full[0], 16)
            partial(as8(0))
            for m in range(4):
                if m == 3:
                    pe.wait_ge(small_ev, 1)
                    pe.wait_ge(c_in, 64)
                    for r in range(2):
                        for t in range(4):
                            tr(psA[:, 2 + r, 128 * t:128 * t + 128], Cr[:, r, t, :])
                    pe.wait_ge(ws_masked, 1)
                    for h in range(NH):
                        tr(psA[:, 1, 128 * h:128 * h + 128], Ws[:, h, :])
                    pe.wait_ge(h0_in, 32)
                    pe.wait_ge(zs_copied, 1)
                    for r in range(2):
                        ins = tr(psA[:, 0, 128 * r:128 * r + 128], h0[:, r, :])
                    ins.then_inc(small_ps, 1)
                for k in range(KD):
                    ins = mm(psB[:, m, :], as8(0)[:, k, 128 * m:128 * m + 128], hnT[:, k, 0:NP_], k == 0, k == KD - 1)
                ins.then_inc(xa_ps, 1)
            pe.wait_ge(small_ev, 2)
            total_T(0)
            pe.wait_ge(w_full[1], 16)
            partial(as8(1))

            def to_T(w, first):
                for m in range(4):
                    if first + m >= 2:
                        pe.wait_ge(in_ev, first + m - 1)
                    for k in range(KD):
                        ins = mm(psA[:, 2 + m % 2, :], w[:, k, 128 * m:128 * m + 128], hnT[:, k, 0:NP_], k == 0, k == KD - 1)
                    ins.then_inc(in_ps, 1)

            to_T(as8(1), 0)
            total_T(1)
            pe.wait_ge(ptst_rdy, 1)
            pe.wait_ge(u_copied, 2)
            for g in range(8):
                if g >= 4:
                    pe.wait_ge(pt_copied, g - 3)
                for j in range(4):
                    q, r = 2 * g + j // 2, j % 2
                    ins = tr(psB[:, g % 4, 128 * j:128 * j + 128], PTst[:, q, r].rearrange("p e n -> p (e n)"))
                ins.then_inc(pt_ps, 1)
            pe.wait_ge(pt_copied, 8)
            pe.wait_ge(qt_rdy, 1)
            for q in range(NQ):
                out = psB[0:32, q // 4, 128 * (q % 4):128 * (q % 4) + 128]
                for r in range(2):
                    ins = mm(out, PTst[:, q, r, 0, :], QT[:, q, r, 0:128], r == 0, r == 1)
            ins.then_inc(m_ps, 1)

            def v_rows(t):
                pe.wait_ge(in_ev, 3 + t)
                for k in range(KD):
                    ins = mm(psA[:, 2 + t % 2, :], hnT[:, k, 128 * t:128 * t + 128], as8(2)[:, k, :], k == 0, k == KD - 1)
                ins.then_inc(in_ps, 1)

            pe.wait_ge(w_full[2], 16)
            partial(as8(2))
            v_rows(0)
            pe.wait_ge(m_copied, 1)
            pe.wait_ge(zT_used, 1)
            for w in range(4):
                for r in range(2):
                    if w:
                        pe.wait_ge(v_copied, 2 * (w - 1) + r + 1)
                    for j in range(4):
                        ins = mm(by_pair(psB)[:, 4 * r + j, 0:UC], PT[:, 4 * w + j, r, :], U[:, 4 * w + j, :], True, True)
                    ins.then_inc(v_ps, 1)
            for t in range(1, 4):
                v_rows(t)
            pe.wait_ge(zs_copied, 3)
            pe.wait_ge(zT_used, 2)
            mm(psA[0:NS, 1, :], sel[:, :], zs, True, True).then_inc(zT_ps, 1)
            pe.wait_ge(w_full[0], 32)
            partial(as8(0))
            to_T(as8(0), 8)
            total_T(3)
            pe.wait_ge(h_rdy, 2)
            tr(psA[0:32, 0, 0:128], hfin[:, :, :].rearrange("p r q -> p (r q)"))
            for r in range(2):
                tr(psA[:, 0, 128 + 128 * r:256 + 128 * r], hnew[:, r].rearrange("p n q -> p (n q)"))
            pe.wait_ge(vbn, NT)
            for h in range(NH):
                ins = tr(psA[:, 0, 384 + NS * h:384 + NS * h + NS], vbs[0:NS, 128 * h:128 * h + 128])
            ins.then_inc(hout_ps, 1)
            for ql in range(4):
                if ql >= 2:
                    pe.wait_ge(y_ev, ql - 1)
                for m in range(4):
                    q = 4 * m + ql
                    out = by_pair(psB)[:, 4 * (ql % 2) + m, 0:YC]
                    mm(out, MT[:, q, :], U[:, q, 0:YC], True, False)
                    mm(out, QT[:, q, 0, 32:160], VH[:, 0, q, 0:YC], False, False)
                    ins = mm(out, QT[:, q, 1, 32:160], VH[:, 1, q, 0:YC], False, True)
                ins.then_inc(y_ps, 1)
            pe.wait_ge(hout_copied, 1)
            pe.wait_ge(in_ev, 12)
            pe.wait_ge(zT_used, 4)
            for h in range(NH):
                for t in range(4):
                    ins = mm(psA[:, h, 128 * t:128 * t + 128], vb[:, t, 128 * h:128 * h + 128], WT[:, h, :], True, True)
                ins.then_inc(s_ps, 1)
            pe.wait_ge(y_ev, 4)

            wo = [as4(1), as4(2)]

            def out_proj(n, t):
                ps = (psB, psA)[t % 2]
                for j in range(2):
                    if j and n >= 2:
                        pe.wait_ge(lg_ev, min(n - 1, 2))
                    for h in range(2):
                        if t == 3 and j and h:
                            pe.wait_ge(o_sc, 1)
                        for k in range(4):
                            if t == 0 and h == 0:
                                pe.wait_ge(yb_rdy if j else ya_rdy, k + 1)
                            ins = mm(ps[:, 2 * j + h, :], mixT[:, 4 * j + k, 128 * t:128 * t + 128],
                                     wo[j][:, k, 512 * h:512 * h + 512], k == 0, k == 3)
                ins.then_inc(o_ps, 1)

            def router(n, t):
                r = ROWS[t]
                ps = (psB, psA)[t % 2]
                pe.wait_ge(o_ev, n + 1)
                pe.wait_ge(hn2_rdy, n + 1)
                cols = hn2[0:r, n % 2, :].rearrange("p (m k) -> p k m", k=KD)
                for k in range(KD):
                    ins = tr(ps[:, k // 4, 128 * (k % 4):128 * (k % 4) + r], cols[:, k])
                ins.then_inc(hn2T_ps, 1)
                pe.wait_ge(hn2T_ev, n + 1)
                if t == 4:
                    pe.wait_ge(lg_ev, 3)
                for k in range(KD):
                    ins = mm(ps[0:r, 2, 0:36], hn2T[:, k, 0:r], wr[:, k, :], k == 0, k == KD - 1)
                ins.then_inc(lg_ps, 1)

            pe.wait_ge(w_full[1], 32)
            pe.wait_ge(w_full[2], 32)
            out_proj(0, 0)
            pe.wait_ge(yb_rdy, 5)
            pe.wait_ge(sq_rdy, 9)
            for k in range(4):
                for j, s in enumerate((sq, sqb)):
                    mm(psA[32 * j:32 * j + 1, 2, :], ones[:, 0:1], s[:, k, 0:NP_], k == 0, k == 3)
            for k in range(4):
                for j, s in enumerate((sq, sqb)):
                    ins = mm(psA[32 * j:32 * j + 1, 3, 0:NS], ones[:, 0:1], s[:, k, NP_:NTOK], k == 0, k == 3)
            ins.then_inc(sum_ps, 1)
            pe.wait_ge(srow_rdy, 1)
            for j in range(2):
                p = slice(32 * j, 32 * j + 1)
                for t in range(4):
                    mm(psA[:, 1 - j, 64 + t:65 + t], srow[p, 128 * t:128 * t + 128], ones[p, 0:1], True, True)
                for g in (2 * j, 2 * j + 1):
                    ins = mm(psA[32 * g:32 * g + NS, 1 - j, 68:69], srow[p, NP_:NTOK], ones[p, 0:1], True, True)
            ins.then_inc(rab_ps, 1)
            pe.wait_ge(rab_ms, 1)
            out_proj(1, 1)
            pe.wait_ge(rest_in, 16 * 6)
            router(0, 0)
            out_proj(2, 2)
            router(1, 1)
            for k in range(4):
                for j in range(2):
                    for h in range(2):
                        g = 2 * j + h
                        ins = mm(psA[32 * g:32 * g + NS, 3, :], mixT[:, 4 * j + k, NP_:NTOK], wo[j][:, k, 512 * h:512 * h + 512], k == 0, k == 3)
            ins.then_inc(o_ps, 1)
            out_proj(4, 3)
            router(2, 2)
            router(3, 4)
            router(4, 3)
            pe.wait_ge(oh_rdy, 1)
            for t in range(NT):
                out = psA[0:ROWS[t], 0, 32 * t:32 * t + 32]
                for s in range(t):
                    mm(out, oneb[:, 0:ROWS[t]], ohb[:, s, :], s == 0, False)
                mm(out, trib[0:ROWS[t], 0:ROWS[t]], ohb[0:ROWS[t], t, :], t == 0, True)
            for t in range(NT):
                ins = mm(psA[:, 1, 0:NE], oneb[0:ROWS[t], :], ohb[0:ROWS[t], t, :], t == 0, t == NT - 1)
            ins.then_inc(pre_ps, 1)

            pe.wait_ge(slot_rdy, 1)
            for n in range(2 * NT):
                r = ROWS[n % NT]
                ins = mm(psA[0:C, 2, 0:2 * NTL], row_oh[0:r, n, :], entry[0:r, n].rearrange("p t w -> p (t w)"), n == 0, n == 2 * NT - 1)
            ins.then_inc(tbl_ps, 1)

            pe.wait_ge(tbl_rdy, 1)

            def x_T(out, x):
                cols = x.rearrange("p (m k) -> p k m", k=KD)
                for k in range(KD):
                    ins = tr(out[:, C * k:C * k + C], cols[:, k])
                return ins

            def gate_up(out, xT, g, up):
                for k in range(KD):
                    gate = early[k // 4][:, k % 4, :] if g is None else as8(g)[:, k, :]
                    mm(out[0:64], xT[:, k, :], gate, k == 0, k == KD - 1)
                    ins = mm(out[64:128], xT[:, k, :], as8(up)[:, k, :], k == 0, k == KD - 1)
                return ins

            def h_T(out, h):
                cols = h.rearrange("p (m k) -> p k m", k=4)
                for k in range(4):
                    ins = tr(out[:, C * k:C * k + C], cols[:, k])
                return ins

            def down(out, hT_, dn):
                for k in range(4):
                    for h in range(2):
                        ins = mm(out[64 * h:64 * h + 64], hT_[:, k, :], as4(dn)[:, k, 512 * h:512 * h + 512], k == 0, k == 3)
                return ins

            def wait_before(signal, count):
                count = count if isinstance(count, int) else pe.to_reg(count)
                pe.wait_ge(slot_rdy, 1)
                pe.wait_ge(signal, count)

            def tile_step(s, i, u, first=False, last=False):
                ps, other = (psA, psB)[u], (psA, psB)[1 - u]
                g, up, dn = EXP_SLOTS[u]
                pe.wait_ge(xgT_ev, s + 1)
                if isinstance(s, int) and s == 2:
                    pe.wait_ge(early_in, 32)
                    g = None
                else:
                    missed = 1 if u == 0 and not first else 0
                    pe.wait_ge(w_full[g], (i + 1 - missed + PRIOR[g]) * 16)
                pe.wait_ge(w_full[up], (i + 1 + PRIOR[up]) * 16)
                gate_up(ps[:, 1, :], xgT[:, u], g, up).then_inc(gu_ps, 1)
                if not first:
                    wait_before(h_done, s)
                    h_T(other[:, 2, :], hh[0:64, 1 - u, :]).then_inc(hT_ps, 1)
                if not last:
                    wait_before(xg_in[1 - u], (i + 1 + u) * 16)
                    x_T(other[:, 0, :], xg[0:C, 1 - u, :]).then_inc(xgT_ps, 1)
                if not first:
                    dnp = EXP_SLOTS[1 - u][2]
                    pe.wait_ge(hT_ev, s)
                    pe.wait_ge(w_full[dnp], (i + u + PRIOR[dnp]) * 16)
                    down(other[:, 3, :], hT[:, 1 - u], dnp).then_inc(dn_ps, 1)
                x0 = pe.value_load(xb[0:1, bass.ds(s, 1)], min_val=0, max_val=NX)
                x1 = pe.value_load(xb[0:1, bass.ds(s + 1, 1)], min_val=0, max_val=NX)
                with pe.If(x0 >= x1):
                    pe.drain().then_inc(gu_used, 1)
                with pe.If(x0 < x1), pe.Fori(x0, x1) as x:
                    wait_before(xx_in, (x + 1) * 16)
                    x_T(ps[:, 0, :], xxg[0:C]).then_inc(xx_T, 1)
                    pe.wait_ge(xx_Tev, x + 1)
                    gate_up(other[:, 1, :], xxgT, g, up).then_inc(xx_gu, 1)
                    with pe.If(x + 1 >= x1):
                        pe.drain().then_inc(gu_used, 1)
                    wait_before(xx_h, x + 1)
                    h_T(other[:, 2, :], xhh[0:64]).then_inc(xx_hT, 1)
                    pe.wait_ge(xx_hTev, x + 1)
                    pe.wait_ge(w_full[dn], (i + 1 + PRIOR[dn]) * 16)
                    if not last:
                        pe.wait_ge(xgT_ev, s + 2)
                    down(other[:, 0, :], xhT, dn).then_inc(xx_dn, 1)
                    pe.wait_ge(xx_y0, x + 1)
                    pe.wait_ge(xx_y1, x + 1)

            pe.wait_ge(xg_in[0], 16)
            x_T(psA[:, 0, :], xg[0:C, 0, :]).then_inc(xgT_ps, 1)
            tile_step(0, 0, 0, first=True)
            tile_step(1, 0, 1)
            tile_step(2, 1, 0)
            with pe.Fori(1, NE // 2 - 1) as i:
                tile_step(i * 2 + 1, i, 1)
                tile_step(i * 2 + 2, i + 1, 0)
            tile_step(NE - 1, NE // 2 - 1, 1, last=True)
            pe.wait_ge(h_done, NE)
            h_T(psB[:, 2, :], hh[0:64, 1, :]).then_inc(hT_ps, 1)
            pe.wait_ge(hT_ev, NE)
            pe.wait_ge(w_full[EXP_SLOTS[1][2]], (NE // 2 + PRIOR[EXP_SLOTS[1][2]]) * 16)
            down(psB[:, 3, :], hT[:, 1], EXP_SLOTS[1][2]).then_inc(dn_ps, 1)


_NAMES = ['x_prompt', 'x_sample', 'state_ssm_re', 'state_ssm_im', 'norm1_g', 'w_in', 'lam_re', 'lam_im', 'log_dt',
          'ssm_b_re', 'ssm_b_im', 'ssm_c_re', 'ssm_c_im', 'ssm_d', 'gmlp_norm_g', 'gmlp_w_s', 'gmlp_b_s',
          'out_norm_ssm_g', 'out_norm_gmlp_g', 'w_out', 'norm2_g', 'w_router_group', 'b_router_group',
          'w_router_expert', 'b_router_expert', 'w_gate', 'w_up', 'w_down', 'final_norm_g']
_OUTS = [(1, NP_, D), (NS, 1, D), (1, 1, 32, 64), (1, 1, 32, 64), (1, NS, 32, 64), (1, NS, 32, 64), (1, NS, 1, DS)]


def kernel(**inputs):
    import numpy as np
    import concourse.bacc as bacc
    from concourse.bass_utils import run_bass_kernel_spmd

    nc = bacc.Bacc("TRN2", target_bir_lowering=False, num_devices=1)
    arrays, args = {}, {}
    for name in _NAMES:
        v = np.ascontiguousarray(inputs[name])
        arrays[f"in_{name}"] = v
        args[name] = nc.dram_tensor(f"in_{name}", v.shape, mybir.dt.from_np(v.dtype), kind="ExternalInput").ap()
    outs = [nc.dram_tensor(f"out_{i}", s, mybir.dt.float32, kind="ExternalOutput").ap() for i, s in enumerate(_OUTS)]
    build(nc, args, outs)
    r = run_bass_kernel_spmd(nc, [arrays], core_ids=[0])
    return tuple(r.results[0][f"out_{i}"] for i in range(len(_OUTS)))
```
